# Optimizing a Trainium2 kernel written in Bass

```python
import jax, jax.numpy as jnp
from jax import lax
import numpy as np

D_MODEL = 1024
BATCH = 1
SEQ = 256
DEPTH = 2

CHUNK = 64
PLE_DIM = 256
EPS = 1e-6
NEG_INF = -1e30

RET_HEADS = 4
RET_QK_DIM = 64
RET_V_DIM = 128
RET_ROPE_THETA = 10000.0

CA_HEADS = 8
CA_HEAD_DIM = 64
CA_BACK_CHUNKS = 8
CA_MAX_REL = 128

SW_Q_HEADS = 16
SW_KV_HEADS = 2
SW_HEAD_DIM = 64
SW_WINDOW = 128
SW_BACK_CHUNKS = SW_WINDOW // CHUNK - 1

ROPE_THETA = 500000.0
ROPE_DIM = SW_HEAD_DIM // 4

MOE_GROUPS = 4
MOE_EXPERTS_PER_GROUP = 4
MOE_TOP_K = 2
MOE_D_FF = 512

N_EVEN = (DEPTH + 1) // 2
N_ODD = DEPTH // 2

EVEN_IN_WIDTH = 2 * RET_HEADS * RET_QK_DIM + 2 * RET_HEADS * RET_V_DIM + 3 * CA_HEADS * CA_HEAD_DIM
EVEN_MIX_WIDTH = RET_HEADS * RET_V_DIM + CA_HEADS * CA_HEAD_DIM
ODD_IN_WIDTH = (SW_Q_HEADS + 2 * SW_KV_HEADS) * SW_HEAD_DIM
ODD_MIX_WIDTH = SW_Q_HEADS * SW_HEAD_DIM

kernel_name = "hybrid_streaming_retention_chunkattn_swa_hmoe"

def rms_norm(x, w):
    xf = x.astype(jnp.float32)
    y = xf * lax.rsqrt(jnp.mean(xf * xf, axis=-1, keepdims=True) + EPS)
    return (y * w.astype(jnp.float32)).astype(x.dtype)

def rope(x, pos, rot_dim, theta):
    half = rot_dim // 2
    inv = theta ** (-jnp.arange(half, dtype=jnp.float32) / half)
    ang = pos.astype(jnp.float32)[:, None] * inv[None, :]
    cos = jnp.cos(ang)[None, :, None, :]
    sin = jnp.sin(ang)[None, :, None, :]
    xr = x[..., :rot_dim].astype(jnp.float32)
    x1, x2 = xr[..., :half], xr[..., half:]
    rot = jnp.concatenate([x1 * cos - x2 * sin, x2 * cos + x1 * sin], axis=-1).astype(x.dtype)
    return jnp.concatenate([rot, x[..., rot_dim:]], axis=-1)

def chunk_band(t, n_back):
    b, s = t.shape[:2]
    nc = s // CHUNK
    rest = t.shape[2:]
    tc = t.reshape((b, nc, CHUNK) + rest)
    pad = jnp.zeros((b, n_back, CHUNK) + rest, t.dtype)
    tp = jnp.concatenate([pad, tc], axis=1)
    idx = jnp.arange(nc)[:, None] + jnp.arange(n_back + 1)[None, :]
    band = tp[:, idx]
    return band.reshape((b, nc, (n_back + 1) * CHUNK) + rest)

def band_mask(nc, n_back):
    valid = (jnp.arange(nc)[:, None] + jnp.arange(n_back + 1)[None, :]) >= n_back
    return jnp.repeat(valid, CHUNK, axis=1)

def retention_chunkwise(q, k, v):
    b, s, h, dk = q.shape
    dv = v.shape[-1]
    nc = s // CHUNK
    log_g = jnp.log(1.0 - 2.0 ** (-5.0 - jnp.arange(h, dtype=jnp.float32)))
    idx = jnp.arange(CHUNK, dtype=jnp.float32)
    intra_decay = jnp.exp(log_g[:, None, None] * jnp.abs(idx[:, None] - idx[None, :]))
    q_decay = jnp.exp(log_g[None, :] * (idx[:, None] + 1.0))
    k_decay = jnp.exp(log_g[:, None] * (CHUNK - 1.0 - idx[None, :]))
    chunk_decay = jnp.exp(log_g * CHUNK)

    qc = q.astype(jnp.float32).reshape(b, nc, CHUNK, h, dk)
    kc = k.astype(jnp.float32).reshape(b, nc, CHUNK, h, dk) * (dk ** -0.5)
    vc = v.astype(jnp.float32).reshape(b, nc, CHUNK, h, dv)

    scores = jnp.einsum('bnihd,bnjhd->bnhij', qc, kc) * intra_decay[None, None]
    inner = jnp.einsum('bnhij,bnjhe->bnihe', scores, vc)

    kv = jnp.einsum('bnjhd,bnjhe,hj->bnhde', kc, vc, k_decay)

    def step(state, kv_n):
        return chunk_decay[None, :, None, None] * state + kv_n, state

    init = jnp.zeros((b, h, dk, dv), jnp.float32)
    _, states = lax.scan(step, init, jnp.moveaxis(kv, 1, 0))
    states = jnp.moveaxis(states, 0, 1)
    cross = jnp.einsum('bnihd,bnhde->bnihe', qc, states) * q_decay[None, None, :, :, None]
    return (inner + cross).reshape(b, s, h, dv)

def chunk_relbias_attention(q, k, v, rel_bias):
    b, s, h, d = q.shape
    nc = s // CHUNK
    band = (CA_BACK_CHUNKS + 1) * CHUNK
    qc = q.reshape(b, nc, CHUNK, h, d)
    kb = chunk_band(k, CA_BACK_CHUNKS)
    vb = chunk_band(v, CA_BACK_CHUNKS)
    sc = jnp.einsum('bnihd,bnjhd->bnhij', qc, kb).astype(jnp.float32) * (d ** -0.5)
    dist = jnp.arange(CHUNK)[:, None] + CA_BACK_CHUNKS * CHUNK - jnp.arange(band)[None, :]
    bucket = jnp.clip(dist, -CA_MAX_REL, CA_MAX_REL) + CA_MAX_REL
    bias = rel_bias[:, bucket].astype(jnp.float32)
    sc = sc + bias[None, None]
    mask = band_mask(nc, CA_BACK_CHUNKS)
    sc = jnp.where(mask[None, :, None, None, :], sc, NEG_INF)
    pr = jax.nn.softmax(sc, axis=-1).astype(v.dtype)
    o = jnp.einsum('bnhij,bnjhd->bnihd', pr, vb)
    return o.reshape(b, s, h * d)

def sliding_window_sink_attention(q, k, v, sinks):
    b, s, hq, d = q.shape
    hkv = k.shape[2]
    g = hq // hkv
    nc = s // CHUNK
    qc = q.reshape(b, nc, CHUNK, hkv, g, d)
    kb = chunk_band(k, SW_BACK_CHUNKS)
    vb = chunk_band(v, SW_BACK_CHUNKS)
    sc = jnp.einsum('bnikgd,bnjkd->bnkgij', qc, kb).astype(jnp.float32) * (d ** -0.5)
    mask = band_mask(nc, SW_BACK_CHUNKS)
    sc = jnp.where(mask[None, :, None, None, None, :], sc, NEG_INF)
    sink_col = jnp.broadcast_to(sinks.astype(jnp.float32).reshape(hkv, g)[None, None, :, :, None, None],
                                sc.shape[:-1] + (1,))
    pr = jax.nn.softmax(jnp.concatenate([sc, sink_col], axis=-1), axis=-1)[..., :-1].astype(v.dtype)
    o = jnp.einsum('bnkgij,bnjkd->bnikgd', pr, vb)
    return o.reshape(b, s, hq * d)

def even_mixer(h, pos, w_in, ret_gn, rel_bias, w_out):
    b, s, _ = h.shape
    proj = h @ w_in
    widths = [RET_HEADS * RET_QK_DIM, RET_HEADS * RET_QK_DIM, RET_HEADS * RET_V_DIM,
              RET_HEADS * RET_V_DIM, CA_HEADS * CA_HEAD_DIM, CA_HEADS * CA_HEAD_DIM,
              CA_HEADS * CA_HEAD_DIM]
    splits = [int(c) for c in np.cumsum(widths)[:-1]]
    rq, rk, rv, rg, aq, ak, av = jnp.split(proj, splits, axis=-1)
    rq = rope(rq.reshape(b, s, RET_HEADS, RET_QK_DIM), pos, RET_QK_DIM, RET_ROPE_THETA)
    rk = rope(rk.reshape(b, s, RET_HEADS, RET_QK_DIM), pos, RET_QK_DIM, RET_ROPE_THETA)
    rv = rv.reshape(b, s, RET_HEADS, RET_V_DIM)
    ro = retention_chunkwise(rq, rk, rv)
    mu = jnp.mean(ro, axis=-1, keepdims=True)
    var = jnp.mean(jnp.square(ro - mu), axis=-1, keepdims=True)
    ro = ((ro - mu) * lax.rsqrt(var + EPS)).reshape(b, s, RET_HEADS * RET_V_DIM)
    ro = ro * ret_gn.astype(jnp.float32)
    ret_out = (jax.nn.silu(rg.astype(jnp.float32)) * ro).astype(h.dtype)
    aq = aq.reshape(b, s, CA_HEADS, CA_HEAD_DIM)
    ak = ak.reshape(b, s, CA_HEADS, CA_HEAD_DIM)
    av = av.reshape(b, s, CA_HEADS, CA_HEAD_DIM)
    att_out = chunk_relbias_attention(aq, ak, av, rel_bias)
    return jnp.concatenate([ret_out, att_out], axis=-1) @ w_out

def odd_mixer(h, pos, w_qkv, b_qkv, sinks, w_out, b_out):
    b, s, _ = h.shape
    proj = h @ w_qkv + b_qkv
    qw = SW_Q_HEADS * SW_HEAD_DIM
    kw = SW_KV_HEADS * SW_HEAD_DIM
    q, k, v = jnp.split(proj, [qw, qw + kw], axis=-1)
    q = rope(q.reshape(b, s, SW_Q_HEADS, SW_HEAD_DIM), pos, ROPE_DIM, ROPE_THETA)
    k = rope(k.reshape(b, s, SW_KV_HEADS, SW_HEAD_DIM), pos, ROPE_DIM, ROPE_THETA)
    v = v.reshape(b, s, SW_KV_HEADS, SW_HEAD_DIM)
    o = sliding_window_sink_attention(q, k, v, sinks)
    return o @ w_out + b_out

def hierarchical_moe(h, w_group, b_group, w_router, b_router, w_gate, w_up, w_down):
    b, s, d = h.shape
    t = h.reshape(b * s, d)
    g_logits = (t @ w_group).astype(jnp.float32) + b_group.astype(jnp.float32)
    g_prob = jax.nn.softmax(g_logits, axis=-1)
    g_idx = jnp.argmax(g_logits, axis=-1)
    g_w = jnp.max(g_prob, axis=-1)
    g_onehot = jax.nn.one_hot(g_idx, MOE_GROUPS, dtype=jnp.float32)
    e_logits = jnp.einsum('td,dge->tge', t, w_router).astype(jnp.float32) + b_router.astype(jnp.float32)
    e_sel = jnp.einsum('tge,tg->te', e_logits, g_onehot)
    top_v, top_i = lax.top_k(e_sel, MOE_TOP_K)
    top_w = jax.nn.softmax(top_v, axis=-1)
    e_gate = jnp.sum(jax.nn.one_hot(top_i, MOE_EXPERTS_PER_GROUP, dtype=jnp.float32) * top_w[..., None], axis=1)
    gates = g_onehot[:, :, None] * (g_w[:, None] * e_gate)[:, None, :]
    out = jnp.zeros_like(t)
    for gi in range(MOE_GROUPS):
        hg = jnp.einsum('td,edf->tef', t, w_gate[gi])
        hu = jnp.einsum('td,edf->tef', t, w_up[gi])
        act = jax.nn.silu(hg) * hu * gates[:, gi, :, None].astype(t.dtype)
        out = out + jnp.einsum('tef,efd->td', act, w_down[gi])
    return out.reshape(b, s, d)

def setup_inputs(seed: int = 0) -> dict:
    key = jax.random.key(seed)
    ks = jax.random.split(key, 24)

    def nrm(k, shape, fan_in):
        return jax.random.normal(k, shape, jnp.float32) * (fan_in ** -0.5)

    def gain(k, shape):
        return 1.0 + 0.05 * jax.random.normal(k, shape, jnp.float32)

    G, E, F = MOE_GROUPS, MOE_EXPERTS_PER_GROUP, MOE_D_FF
    return {
        "x": jax.random.normal(ks[0], (BATCH, SEQ, D_MODEL), jnp.float32),
        "p": jax.random.normal(ks[1], (DEPTH, BATCH, SEQ, PLE_DIM), jnp.float32),
        "norm_mix": gain(ks[2], (DEPTH, D_MODEL)),
        "norm_ffn": gain(ks[3], (DEPTH, D_MODEL)),
        "norm_ple": gain(ks[4], (DEPTH, D_MODEL)),
        "final_norm": gain(ks[5], (D_MODEL,)),
        "even_w_in": nrm(ks[6], (N_EVEN, D_MODEL, EVEN_IN_WIDTH), D_MODEL),
        "even_ret_gn": gain(ks[7], (N_EVEN, RET_HEADS * RET_V_DIM)),
        "even_rel_bias": 0.2 * jax.random.normal(ks[8], (N_EVEN, CA_HEADS, 2 * CA_MAX_REL + 1), jnp.float32),
        "even_w_out": nrm(ks[9], (N_EVEN, EVEN_MIX_WIDTH, D_MODEL), EVEN_MIX_WIDTH),
        "odd_w_qkv": nrm(ks[10], (N_ODD, D_MODEL, ODD_IN_WIDTH), D_MODEL),
        "odd_b_qkv": 0.02 * jax.random.normal(ks[11], (N_ODD, ODD_IN_WIDTH), jnp.float32),
        "odd_sinks": 0.5 * jax.random.normal(ks[12], (N_ODD, SW_Q_HEADS), jnp.float32),
        "odd_w_out": nrm(ks[13], (N_ODD, ODD_MIX_WIDTH, D_MODEL), ODD_MIX_WIDTH),
        "odd_b_out": 0.02 * jax.random.normal(ks[14], (N_ODD, D_MODEL), jnp.float32),
        "moe_w_group": nrm(ks[15], (DEPTH, D_MODEL, G), D_MODEL),
        "moe_b_group": 0.01 * jax.random.normal(ks[16], (DEPTH, G), jnp.float32),
        "moe_w_router": nrm(ks[17], (DEPTH, D_MODEL, G, E), D_MODEL),
        "moe_b_router": 0.01 * jax.random.normal(ks[18], (DEPTH, G, E), jnp.float32),
        "moe_w_gate": nrm(ks[19], (DEPTH, G, E, D_MODEL, F), D_MODEL),
        "moe_w_up": nrm(ks[20], (DEPTH, G, E, D_MODEL, F), D_MODEL),
        "moe_w_down": nrm(ks[21], (DEPTH, G, E, F, D_MODEL), F),
        "ple_w_proj": nrm(ks[22], (DEPTH, PLE_DIM, D_MODEL), PLE_DIM),
        "ple_w_gate": nrm(ks[23], (DEPTH, D_MODEL, D_MODEL), D_MODEL),
    }

def reference(x, p, norm_mix, norm_ffn, norm_ple, final_norm,
              even_w_in, even_ret_gn, even_rel_bias, even_w_out,
              odd_w_qkv, odd_b_qkv, odd_sinks, odd_w_out, odd_b_out,
              moe_w_group, moe_b_group, moe_w_router, moe_b_router,
              moe_w_gate, moe_w_up, moe_w_down, ple_w_proj, ple_w_gate):
    pos = jnp.arange(x.shape[1])
    h = x
    for i in range(DEPTH):
        hn = rms_norm(h, norm_mix[i])
        if i % 2 == 0:
            j = i // 2
            mix = even_mixer(hn, pos, even_w_in[j], even_ret_gn[j], even_rel_bias[j], even_w_out[j])
        else:
            j = i // 2
            mix = odd_mixer(hn, pos, odd_w_qkv[j], odd_b_qkv[j], odd_sinks[j], odd_w_out[j], odd_b_out[j])
        h = h + mix
        h = h + hierarchical_moe(rms_norm(h, norm_ffn[i]), moe_w_group[i], moe_b_group[i],
                                 moe_w_router[i], moe_b_router[i],
                                 moe_w_gate[i], moe_w_up[i], moe_w_down[i])
        gate = jax.nn.sigmoid(rms_norm(h, norm_ple[i]) @ ple_w_gate[i])
        h = h + gate * (p[i] @ ple_w_proj[i])
    return rms_norm(h, final_norm)


_drawn_inputs = setup_inputs


def setup_inputs(seed=0):
    import zlib

    import numpy as np

    out = dict(_drawn_inputs(seed))
    spreads = {}
    factors = {'norm_ple': 3.366,
     'odd_b_qkv': 2.683,
     'odd_sinks': 8.0,
     'moe_b_group': 4.276,
     'moe_b_router': 7.79}
    for name, (base, spread) in spreads.items():
        noise = np.random.default_rng([zlib.crc32(name.encode()), seed]).standard_normal(out[name].shape)
        drawn = base * np.exp(spread * noise) if base else spread * noise
        out[name] = __import__('jax').numpy.asarray(drawn.astype(out[name].dtype))
    for name, factor in factors.items():
        out[name] = (out[name] * factor).astype(out[name].dtype)
    return out
```

```python
from contextlib import ExitStack

import numpy as np

import concourse.bass as bass
from concourse import mybir

F32 = mybir.dt.float32
I32 = mybir.dt.int32
ALU = mybir.AluOpType
ACT = mybir.ActivationFunctionType
AX = mybir.AxisListType

P = 128
D = 1024
KD = D // P
SEQ = 256
TT = SEQ // P
EPS = 1e-6
NEG = -1e30
CHUNK = 64

RH, RV = 4, 128
CH = 8
HD = 64
SH, SKV = 16, 2
ROT = 16
MAXREL = 128
REL_W = 3 * P - 1
G, E = 4, 4
NE = G * E
FF = 512
KF = FF // P
PD = 256

BLK = 64
SLOTS = 2 * SEQ
SPAD = SLOTS + BLK
MAXB = 32

NSLOT = 9
UN = 4096

U_IN, U_OUT0 = 0, 6
U_MOE0 = 8
U_PLE0 = U_MOE0 + 3 * NE
U_QKV, U_OUT1 = U_PLE0 + 3, U_PLE0 + 6
U_MOE1 = U_OUT1 + 2
U_PLE1 = U_MOE1 + 3 * NE

C_ID, C_LOW, C_ONE, C_M0, C_M1 = 0, 128, 256, 384, 512
C_COSR, C_SINR, C_COSO, C_SINO, C_REV = 704, 832, 960, 992, 1024
C_N = 1028


def constants():
    c = np.zeros((P, C_N), np.float32)
    i = np.arange(P)
    c[:, C_ID:C_ID + P] = np.eye(P)
    c[:, C_LOW:C_LOW + P] = i[:, None] < i[None, :]
    c[:, C_ONE:C_ONE + P] = 1.0
    first = i < CHUNK
    c[:, C_M0:C_M0 + P] = np.where(first[:, None] & ~first[None, :], NEG, 0.0)
    j = np.arange(192)
    c[:, C_M1:C_M1 + 192] = np.where(first[:, None], (j >= 128)[None, :], (j < 64)[None, :]) * np.float32(NEG)

    def rotary(dim, theta):
        half = dim // 2
        inv = np.float32(theta) ** (-np.arange(half, dtype=np.float32) / np.float32(half))
        ang = (np.arange(SEQ, dtype=np.float32)[:, None] * inv[None, :]).astype(np.float32)
        co, si = np.cos(ang), np.sin(ang)
        tile = lambda a: a.reshape(TT, P, dim).transpose(1, 0, 2).reshape(P, TT * dim)
        return tile(np.concatenate([co, co], 1)), tile(np.concatenate([-si, si], 1))

    c[:, C_COSR:C_COSR + 128], c[:, C_SINR:C_SINR + 128] = rotary(64, 10000.0)
    c[:, C_COSO:C_COSO + 32], c[:, C_SINO:C_SINO + 32] = rotary(ROT, 500000.0)
    c[:, C_REV:C_REV + 4] = [4, 3, 2, 1]
    dec = np.zeros((P, RH, SEQ), np.float64)
    q = np.arange(SEQ)
    for n, h in enumerate((0, 2, 1, 3)):
        g = 1.0 - 2.0 ** (-5.0 - h)
        seen = (q // CHUNK)[None, :] >= (i // CHUNK)[:, None]
        dec[:, n] = np.where(seen, g ** np.abs(q[None, :] - i[:, None]), 0.0) * HD ** -0.5
    return c, dec.reshape(P, RH * SEQ).astype(np.float32)


def bcast(row):
    return bass.AP(row.tensor, row.offset, [[0, P], *[list(d) for d in row.ap[1:]]])


def toeplitz(rel_rows):
    return bass.AP(rel_rows.tensor, 0, [[1, P], [REL_W, CH], [1, 2 * P]])


def head0(g, i):
    return g + 2 * i if g < 2 else (g - 2) // 2 + 2 * (2 * ((g - 2) % 2) + i)


def odd_heads(g):
    if g < 4:
        return 0, [g % 2 + 2 * (4 * (g // 2) + i) for i in range(4)]
    return 1, [(g - 4) % 2 + 2 * (2 * ((g - 4) // 2) + i) for i in range(2)]


def build(nc, x, p, norm_mix, norm_ffn, norm_ple, final_norm, even_w_in, even_ret_gn, even_rel_bias, even_w_out,
          odd_w_qkv, odd_b_qkv, odd_sinks, odd_w_out, odd_b_out, moe_w_group, moe_b_group, moe_w_router,
          moe_b_router, moe_w_gate, moe_w_up, moe_w_down, ple_w_proj, ple_w_gate, const, decay, flip, out, rel_rows):
    wg_d = moe_w_gate.rearrange("l g e d f -> (l g e) d f")
    wu_d = moe_w_up.rearrange("l g e d f -> (l g e) d f")
    wd_d = moe_w_down.rearrange("l g e f d -> (l g e) f d")

    with ExitStack() as ctx:
        def sb(name, shape, dt=F32):
            return ctx.enter_context(nc.sbuf_tensor(name, shape, dt))

        named = {}

        def sem(name):
            if name not in named:
                named[name] = ctx.enter_context(nc.semaphore(name))
            return named[name]

        W = sb("weights", [P, NSLOT, UN])
        H = sb("residual", [P, TT, D])
        XB = sb("normalised", [P, 2 * TT * D])
        AR = sb("arena", [P, 8192])
        C = sb("constants", [P, C_N])
        NW = sb("norm_weights", [P, 6, KD])
        GN = sb("ret_gn", [P, 4])
        WR = sb("router_weights", [P, 2, KD, 20])
        BR = sb("router_bias", [P, 2, 20])
        SK = sb("sinks", [P, SH])
        ST = sb("norm_stats", [P, 8])
        HALF = sb("minus_half", [P, 8])
        RT = sb("router_temps", [P, 420])
        TBL = sb("block_table", [1, 17 + MAXB], I32)
        SM = RT[:, 80:144].rearrange("p (n h) -> p n h", n=4)
        ES = RT[:, 144:176].rearrange("p (t h) -> p t h", t=TT)
        B = [ctx.enter_context(nc.psum_tensor(f"bank{n}", [P, 512], F32)) for n in range(8)]

        HS = XB[:, 0:TT * D].rearrange("p (t d) -> p t d", t=TT)
        XT = XB[:, TT * D:].rearrange("p (k s) -> p k s", k=KD)
        ident = C[:, C_ID:C_ID + P]

        def ar(a, b):
            return AR[:, a:b]

        SCR = W[:, 7:9, :].rearrange("p s n -> p (s n)")
        AQT = ar(0, 1024).rearrange("p (c s) -> p c s", c=4)
        AKT = ar(1024, 2048).rearrange("p (c s) -> p c s", c=4)
        AV = ar(2048, 3072).rearrange("p (t n) -> p t n", t=TT)
        RT4 = ar(3072, 4096).rearrange("p (c s) -> p c s", c=4)
        RVV = ar(4096, 5120).rearrange("p (t n) -> p t n", t=TT)
        GATE = ar(5120, 6144).rearrange("p (t n) -> p t n", t=TT)
        MIXA = ar(6144, 7168).rearrange("p (t n) -> p t n", t=TT)
        RET = ar(7168, 8192).rearrange("p (t n) -> p t n", t=TT)
        RP0 = ar(0, 1024).rearrange("p (h s) -> p h s", h=RH)
        RP1 = ar(1024, 1536).rearrange("p (h s) -> p h s", h=RH)
        STG = [XB[:, n * 1024:(n + 1) * 1024].rearrange("p (t n) -> p t n", t=TT) for n in range(2)]
        REL = AR[0:CH, 7168:7168 + 768]
        TOEP = ar(0, 2048)
        FLIP = ar(2048, 2048 + P)
        BIAS = SCR[:, 0:2048].rearrange("p (h s) -> p h s", h=CH)
        DEC = SCR[:, 2048:3072].rearrange("p (h s) -> p h s", h=RH)
        SC0 = [SCR[:, 3072 + 512 * n:3584 + 512 * n] for n in range(2)]
        PT0 = [SCR[:, 4096 + 512 * n:4608 + 512 * n] for n in range(2)]
        RRO = SCR[:, 5120:6144].rearrange("p (t n) -> p t n", t=TT)
        RTB = SCR[:, 6144:7168].rearrange("p (t n) -> p t n", t=TT)
        THR = SCR[:, 7168:8192].rearrange("p (t n) -> p t n", t=TT)
        BNS = RT[:, 0:48].rearrange("p (t h n) -> p t h n", t=TT, h=RH)
        BNA = RT[:, 48:64].rearrange("p (t h n) -> p t h n", t=TT, h=RH)
        BNE = RT[:, 64:72]
        BNR = RT[:, 72:80]

        Q1 = ar(0, 2048).rearrange("p (t n) -> p t n", t=TT)
        Q1T = ar(2048, 4096).rearrange("p (c s) -> p c s", c=8)
        KV = ar(4096, 4608).rearrange("p (t n) -> p t n", t=TT)
        KDUP = ar(4608, 5120).rearrange("p (t g r n) -> p t g r n", t=TT, g=SKV, r=2)
        K1T = ar(5120, 5632).rearrange("p (g s) -> p g s", g=SKV)
        BQ = ar(5632, 6912)
        BO = ar(5632, 6656)
        RB1 = ar(6912, 7488).rearrange("p (t h n) -> p t h n", t=TT, h=SH + SKV)
        SC1 = [ar(512 * n, 512 * n + 512) for n in range(2)]
        PT1 = [ar(1024 + 512 * n, 1536 + 512 * n) for n in range(2)]
        MIX1 = HS

        PH = ar(0, 2 * SPAD).rearrange("p (t s) -> p t s", t=TT)
        YT = ar(1152, 1152 + KD * SPAD).rearrange("p (k s) -> p k s", k=KD)
        IOTA = ar(1152, 1152 + SPAD)
        GM = ar(1728, 1728 + 2 * SPAD).rearrange("p (t s) -> p t s", t=TT)
        TMP = ar(2880, 2880 + 2 * SPAD).rearrange("p (t s) -> p t s", t=TT)
        GRID = [ar(4032 + 512 * n, 4544 + 512 * n) for n in range(3)]
        GT = ar(5760, 6784).rearrange("p (s t) -> p s t", s=4)
        XBLK = ar(6784, 7296).rearrange("p (k s) -> p k s", k=KD)
        ACTT = ar(7296, 7552)
        TH = ar(7552, 7808)
        AG = ar(7808, 8064)
        PBLK = ar(8064, 8192).rearrange("p (t s) -> p t s", t=TT)
        YS = XB[:, :].rearrange("p (s d) -> p s d", s=4)

        PIN = ar(0, 512).rearrange("p (t n) -> p t n", t=TT)
        PINT = ar(512, 1024).rearrange("p (k s) -> p k s", k=2)
        THG = ar(1024, 3072).rearrange("p (t n) -> p t n", t=TT)
        FW = ar(3072, 4096)
        OUTB = ar(4096, 6144).rearrange("p (t n) -> p t n", t=TT)

        def unit(n):
            return W[:, n % NSLOT, :]

        def landed(n):
            return sem(f"slot{n % NSLOT}_landed"), 16 * (n // NSLOT + 1)

        block = ctx.enter_context(nc.Block())

        @block.sync
        def _(sp):
            def put(n, dst, src):
                if n >= NSLOT:
                    sp.wait_ge(sem("units_used"), n - NSLOT + 1)
                sp.dma_start(dst, src).then_inc(landed(n)[0], 16)

            def cols(n, w, a, width=512):
                put(n, unit(n)[:, 0:KD * width].rearrange("p (k n) -> p k n", k=KD),
                    w[:, a:a + width].rearrange("(p k) n -> p k n", p=P))

            def rows(n, w, a):
                put(n, unit(n).rearrange("p (k n) -> p k n", k=KD), w[:, a:a + 512].rearrange("(k p) n -> p k n", p=P))

            def expert(layer, u0):
                srcs = (wg_d, wu_d, wd_d)

                def three(e, value, used):
                    for m in range(3):
                        used(m)
                        n = value + m
                        s = srcs[m][e]
                        src = s.rearrange("(p k) f -> p (k f)", p=P) if m < 2 else s.rearrange("(k p) d -> p k d", p=P)
                        dst = unit(n) if m < 2 else unit(n).rearrange("p (k d) -> p k d", k=KF)
                        sp.dma_start(dst, src).then_inc(landed(n)[0], 16)

                def first(m):
                    if u0 + m >= NSLOT:
                        sp.wait_ge(sem("units_used"), u0 + m - NSLOT + 1)

                three(layer * NE, u0, first)
                with sp.Fori(0, 5) as i:
                    for j in range(3):
                        n = u0 + 3 + 3 * j
                        three(i * 3 + (layer * NE + 1 + j), n,
                              lambda m: sp.wait_ge(sem("units_used"), i * 9 + (n + m - NSLOT + 1)))

            sp.dma_start(H[:, :, :], x[0].rearrange("(t p) d -> p t d", p=P)).then_inc(sem("x_landed"), 16)
            sp.dma_start(C[:, :], const).then_inc(sem("const_landed"), 16)
            order = [1536, 2048, 2560, 0, 512, 1024]
            for u in range(6):
                cols(U_IN + u, even_w_in[0], order[u])
            rows(U_OUT0, even_w_out[0], 0)
            sp.wait_ge(sem("ret_out"), 2)
            rows(U_OUT0 + 1, even_w_out[0], 512)
            expert(0, U_MOE0)

            def ple(l, n):
                put(n, unit(n)[:, 0:2 * D].rearrange("p (k n) -> p k n", k=2),
                    ple_w_proj[l].rearrange("(k p) n -> p k n", p=P))
                for c in range(2):
                    cols(n + 1 + c, ple_w_gate[l], 512 * c)

            ple(0, U_PLE0)
            cols(U_QKV, odd_w_qkv[0], 0)
            cols(U_QKV + 1, odd_w_qkv[0], 512)
            cols(U_QKV + 2, odd_w_qkv[0], 1024, 256)
            rows(U_OUT1, odd_w_out[0], 0)
            rows(U_OUT1 + 1, odd_w_out[0], 512)
            expert(1, U_MOE1)
            ple(1, U_PLE1)
            sp.wait_ge(sem("out_ready"), 2)
            sp.dma_start(out[0].rearrange("(t p) d -> p t d", p=P), OUTB).then_inc(sem("stored"), 16)
            sp.wait_ge(sem("stored"), 16)

        @block.gpsimd
        def _(pool):
            pool.memset(HALF[:, :], -0.5).then_inc(sem("half_set"), 1)
            small = sem("small_landed")
            for n, w in enumerate((norm_mix, norm_ffn, norm_ple)):
                for l in range(2):
                    pool.dma_start(NW[:, 3 * l + n, :], w[l].rearrange("(p k) -> p k", p=P)).then_inc(small, 16)
            pool.dma_start(GN[:, :], even_ret_gn[0].rearrange("(c p) -> p c", p=P),
                           allow_slow_non_contiguous=True).then_inc(small, 16)
            for l in range(2):
                pool.dma_start(WR[:, l, :, 0:4], moe_w_group[l].rearrange("(p k) g -> p k g", p=P)).then_inc(small, 16)
                pool.dma_start(WR[:, l, :, 4:20],
                               moe_w_router[l].rearrange("(p k) g e -> p k (g e)", p=P)).then_inc(small, 16)
                pool.dma_start(BR[:, l, 0:4], bcast(moe_b_group[l:l + 1, :])).then_inc(small, 16)
                pool.dma_start(BR[:, l, 4:20], bcast(moe_b_router[l:l + 1].rearrange("l g e -> l (g e)")))\
                    .then_inc(small, 16)
            pool.dma_start(SK[:, :], bcast(odd_sinks)).then_inc(small, 16)

            def power(k):
                pool.wait_ge(sem("ms_ready"), k + 1)
                pool.tensor_tensor(ST[:, 4:6], ST[:, 2:4], HALF[:, 0:2], ALU.pow).then_inc(sem("rstd_ready"), 1)

            def patterns(l):
                pool.wait_ge(sem("xT_by_dve"), 2 * (3 * l + 2))
                pool.iota(IOTA, [[1, SPAD]], base=0, channel_multiplier=0,
                          allow_small_or_imprecise_dtypes=True).then_inc(sem("iota_ready"), 1)
                pool.iota(GRID[0], [[1, MAXB], [0, NE]], base=0, channel_multiplier=0,
                          allow_small_or_imprecise_dtypes=True).then_inc(sem("iota_ready"), 1)

            pool.wait_ge(sem("half_set"), 1)
            power(0)
            pool.wait_ge(sem("gn_ready"), 1)
            pool.tensor_tensor(BNR, BNE, HALF[:, 0:8], ALU.pow).then_inc(sem("gn_rstd"), 1)
            power(1)
            patterns(0)
            power(2)
            power(3)
            power(4)
            patterns(1)
            power(5)
            power(6)

        @block.tensor
        def _(pe):
            def transposes(k):
                for q in range(4):
                    for kk in range(2):
                        for t in range(TT):
                            if q == 0 and kk == 0:
                                pe.wait_ge(sem("hs_ready"), 2 * k + t + 1)
                            mm = pe.transpose(B[4 + q][:, kk * SEQ + t * P:kk * SEQ + (t + 1) * P],
                                              HS[:, t, 2 * q + kk:D:KD], ident)
                    mm.then_inc(sem("hT_ready"), 1)

            def xt_ready(k):
                pe.wait_ge(sem("xT_by_dve"), 2 * (k + 1))
                pe.wait_ge(sem("xT_by_act"), 2 * (k + 1))

            def project(n, banks, left, width=512, free=None, done=None, t_free=None):
                s, v = landed(n)
                pe.wait_ge(s, v)
                w = unit(n)[:, 0:KD * width].rearrange("p (k n) -> p k n", k=KD)
                for t in range(TT):
                    if free is not None:
                        free(t)
                    for k in range(KD):
                        mm = pe.matmul(B[banks[t]][:, 0:width], left[:, k, t * P:(t + 1) * P], w[:, k, :],
                                       start=(k == 0), stop=(k == KD - 1))
                    mm.then_inc(sem(done), 1)
                pe.drain().then_inc(sem("units_used"), 1)

            pe.wait_ge(sem("const_landed"), 16)
            transposes(0)
            xt_ready(0)

            def in_unit(u):
                def free(t):
                    if u >= 2:
                        pe.wait_ge(sem("in_by_dve" if t == 0 else "in_by_act"), u - 1)
                project(U_IN + u, (2 * (u % 2), 2 * (u % 2) + 1), XT, free=free, done="in_ready")

            def turn(src, banks, name):
                for c in range(4):
                    for t in range(TT):
                        mm = pe.transpose(B[banks[c // 2]][:, (c % 2) * SEQ + t * P:(c % 2) * SEQ + (t + 1) * P],
                                          src[:, t, c * P:(c + 1) * P], ident)
                    if c % 2:
                        mm.then_inc(sem(name), 1)

            def even_group(g):
                return (0, [head0(g, i) for i in range(4)], 128) if g < 2 else (1, [head0(g, i) for i in range(2)], 256)

            def scores0(g):
                t, heads, keys = even_group(g)
                if g >= 2:
                    pe.wait_ge(sem("s0_scaled"), g - 1)
                for i, h in enumerate(heads):
                    r = 64 * (h % 2)
                    mm = pe.matmul(B[4 + g % 2][:, i * keys:(i + 1) * keys], AQT[r:r + 64, h // 2, t * P:(t + 1) * P],
                                   AKT[r:r + 64, h // 2, 0:keys], start=True, stop=True)
                mm.then_inc(sem("s0_ready"), 1)

            def probs0(g):
                pe.wait_ge(sem("s0_exp"), sum(len(even_group(n)[1]) for n in range(g + 1)))
                if g >= 1:
                    pe.wait_ge(sem("pt0_copied"), g)
                for i in range(4):
                    mm = pe.transpose(B[6][:, i * P:(i + 1) * P], SC0[g % 2][:, i * P:(i + 1) * P], ident)
                mm.then_inc(sem("pt0_ready"), 1)

            def values0(g):
                t, heads, keys = even_group(g)
                pe.wait_ge(sem("pt0_copied"), g + 1)
                if g == 2:
                    pe.wait_ge(sem("att0_out"), 1)
                kt = keys // P
                for i, h in enumerate(heads):
                    for n in range(kt):
                        mm = pe.matmul(B[7][:, h * HD:(h + 1) * HD], PT0[g % 2][:, (i * kt + n) * P:(i * kt + n + 1) * P],
                                       AV[:, n, h * HD:(h + 1) * HD], start=(n == 0), stop=(n == kt - 1))
                mm.then_inc(sem("pv0_ready"), 1)

            in_unit(0)
            pe.wait_ge(sem("bias_landed"), 32)
            for n in range(4):
                pe.matmul(B[4 + n][:, :], FLIP, TOEP[:, n * 512:(n + 1) * 512], start=True, stop=True)\
                    .then_inc(sem("bias_ready"), 1)
            in_unit(1)
            pe.wait_ge(sem("bias_copied"), 4)
            pe.wait_ge(sem("in_by_dve"), 1)
            pe.wait_ge(sem("in_by_act"), 1)
            turn(STG[0], (4, 5), "aqk_turned")
            pe.wait_ge(sem("in_by_dve"), 2)
            pe.wait_ge(sem("in_by_act"), 2)
            turn(STG[1], (6, 7), "aqk_turned")
            in_unit(2)
            pe.wait_ge(sem("aqkT_by_dve"), 2)
            pe.wait_ge(sem("aqkT_by_act"), 2)
            scores0(0)
            scores0(1)
            in_unit(3)
            pe.wait_ge(sem("in_by_dve"), 3)
            pe.wait_ge(sem("in_by_act"), 3)
            probs0(0)
            scores0(2)
            probs0(1)
            values0(0)
            scores0(3)
            in_unit(4)
            values0(1)
            probs0(2)
            scores0(4)
            probs0(3)
            values0(2)
            scores0(5)
            in_unit(5)
            values0(3)
            probs0(4)
            probs0(5)
            values0(4)
            values0(5)
            pe.wait_ge(sem("ret_rotated"), 2)
            turn(RRO, (4, 5), "rqk_turned")
            pe.wait_ge(sem("rqkT_by_dve"), 1)
            pe.wait_ge(sem("rqkT_by_act"), 1)
            pe.wait_ge(sem("pt0_copied"), 6)
            pe.wait_ge(sem("att0_out"), 2)
            for par in range(2):
                r = 64 * par
                for i in range(2):
                    mm = pe.matmul(B[4 + par][:, i * SEQ:(i + 1) * SEQ], RT4[r:r + 64, 2 + i, 0:P], RT4[r:r + 64, i, :],
                                   start=True, stop=True)
                mm.then_inc(sem("rs_ready"), 1)
            for par in range(2):
                r = 64 * par
                for i in range(2):
                    mm = pe.matmul(B[6 + par][:, i * P:(i + 1) * P], RT4[r:r + 64, 2 + i, P:SEQ], RT4[r:r + 64, i, P:SEQ],
                                   start=True, stop=True)
                mm.then_inc(sem("rs_ready"), 1)
            pe.wait_ge(sem("rs_decayed"), 4)
            pe.wait_ge(sem("in_by_dve"), 5)
            pe.wait_ge(sem("in_by_act"), 5)
            for t in range(TT):
                for n in range(RH):
                    h = (0, 2, 1, 3)[n]
                    dst, v = B[t][:, h * RV:(h + 1) * RV], slice(h * RV, (h + 1) * RV)
                    mm = pe.matmul(dst, RP0[:, n, t * P:(t + 1) * P], RVV[:, 0, v], start=True, stop=(t == 0))
                    if t:
                        mm = pe.matmul(dst, RP1[:, n, :], RVV[:, 1, v], start=False, stop=True)
                mm.then_inc(sem("ro_ready"), 1)
            turn(MIXA, (6, 7), "mix0_turned")
            pe.wait_ge(sem("ret_out"), 2)
            turn(RET, (4, 5), "mix0_turned")
            pe.wait_ge(sem("mix0T_by_dve"), 2)
            pe.wait_ge(sem("mix0T_by_act"), 2)
            project(U_OUT0, (0, 1), XT, done="out0_ready")
            project(U_OUT0 + 1, (2, 3), XT, done="out0_ready")

            def experts(l, u0):
                kn = 3 * l + 1
                transposes(kn)
                xt_ready(kn)
                if l == 0:
                    pe.wait_ge(sem("small_landed"), 16 * 16)
                for t in range(TT):
                    for k in range(KD):
                        mm = pe.matmul(B[0][:, t * 20:(t + 1) * 20], XT[:, k, t * P:(t + 1) * P], WR[:, l, k, :],
                                       start=(k == 0), stop=(k == KD - 1))
                mm.then_inc(sem("logits_ready"), 1)
                pe.wait_ge(sem("chosen"), l + 1)
                M = RT[:, 100:132].rearrange("p (t e) -> p t e", t=TT)
                low, one = C[:, C_LOW:C_LOW + P], C[:, C_ONE:C_ONE + P]
                pe.matmul(B[1][:, 0:NE], low, M[:, 0, :], start=True, stop=True)
                pe.matmul(B[1][:, NE:2 * NE], one, M[:, 0, :], start=True, stop=False)
                pe.matmul(B[1][:, NE:2 * NE], low, M[:, 1, :], start=False, stop=True)
                pe.matmul(B[1][:, 2 * NE:3 * NE], one, M[:, 0, :], start=True, stop=False)
                pe.matmul(B[1][:, 2 * NE:3 * NE], one, M[:, 1, :], start=False, stop=True).then_inc(sem("ranks_ready"), 1)

                def gather():
                    for k in range(KD):
                        for t in range(TT):
                            mm = pe.matmul(B[4][:, k * BLK:(k + 1) * BLK], HS[:, t, k:D:KD], PBLK[:, t, :],
                                           start=(t == 0), stop=(t == TT - 1))
                    mm.then_inc(sem(f"rows{l}_ready"), 1)

                pe.wait_ge(sem(f"pblk{l}_ready"), 1)
                gather()
                pe.wait_ge(sem("gates_ready"), l + 1)
                for s in range(4):
                    for t in range(TT):
                        mm = pe.transpose(B[6 + s // 2][:, (s % 2) * SEQ + t * P:(s % 2) * SEQ + (t + 1) * P],
                                          GM[:, t, s * P:(s + 1) * P], ident)
                mm.then_inc(sem("gates_turned"), 1)

                pe.wait_ge(sem("table_ready"), 2 * (l + 1))

                def expert(e, n, lap):
                    b0 = pe.value_load(TBL[0:1, bass.ds(e, 1)], min_val=0, max_val=MAXB - 1)
                    b1 = pe.value_load(TBL[0:1, bass.ds(e + 1, 1)], min_val=1, max_val=MAXB - 1)
                    wg, wu = (unit(n + m).rearrange("p (k f) -> p k f", k=KD) for m in range(2))
                    wd = unit(n + 2).rearrange("p (k d) -> p k d", k=KF)

                    def arrived(m):
                        s, v = landed(n + m)
                        pe.wait_ge(s, v if lap is None else lap * 16 + v)

                    with pe.Fori(b0, b1) as b:
                        arrived(0)
                        pe.wait_ge(sem(f"xblk{l}_ready"), b + 1)
                        for m, w in enumerate((wg, wu)):
                            if m == 1:
                                arrived(1)
                            for f in range(KF):
                                for k in range(KD):
                                    mm = pe.matmul(B[2 + m][:, f * BLK:(f + 1) * BLK], w[:, k, f * P:(f + 1) * P],
                                                   XBLK[:, k, :], start=(k == 0), stop=(k == KD - 1))
                            mm.then_inc(sem(f"gu{l}_ready"), 1)
                        pe.wait_ge(sem(f"pblk{l}_ready"), b + 2)
                        gather()
                        arrived(2)
                        pe.wait_ge(sem(f"act{l}_ready"), b + 1)
                        pe.wait_ge(sem(f"y{l}_free"), b + 1)
                        for c in range(KD):
                            for f in range(KF):
                                mm = pe.matmul(B[5][:, c * BLK:(c + 1) * BLK], wd[:, f, c * P:(c + 1) * P],
                                               ACTT[:, f * BLK:(f + 1) * BLK], start=(f == 0), stop=(f == KF - 1))
                        mm.then_inc(sem(f"y{l}_ready"), 1)
                    pe.drain().then_inc(sem("units_used"), 3)

                expert(0, u0, None)
                with pe.Fori(0, 5) as i:
                    for j in range(3):
                        expert(i * 3 + (1 + j), u0 + 3 + 3 * j, i)

                nb = pe.value_load(TBL[0:1, 16:17], min_val=1, max_val=MAXB - 1)
                pe.wait_ge(sem(f"y{l}_free"), nb + 1)
                pe.wait_ge(sem(f"xblk{l}_ready"), nb + 1)
                pe.wait_ge(sem("gates_copied"), 2 * (l + 1))
                for s in range(4):
                    for half in range(2):
                        bank = 4 + (2 * s + half) % 4
                        if s >= 2:
                            pe.wait_ge(sem("ys_by_dve" if half == 0 else "ys_by_act"), 4 * l + s - 1)
                        for c in range(4):
                            mm = pe.transpose(B[bank][:, c * P:(c + 1) * P], YT[:, 4 * half + c, s * P:(s + 1) * P], ident)
                        mm.then_inc(sem("ys_ready"), 1)
                for s in range(4):
                    pe.wait_ge(sem("ys_by_dve"), 4 * l + s + 1)
                    pe.wait_ge(sem("ys_by_act"), 4 * l + s + 1)
                    for t in range(TT):
                        for half in range(2):
                            mm = pe.matmul(B[2 * t + half][:, :], GT[:, s, t * P:(t + 1) * P],
                                           YS[:, s, half * 512:(half + 1) * 512], start=(s == 0), stop=(s == 3))
                            if s == 3:
                                mm.then_inc(sem("moe_ready"), 1)

            def ple(l, n):
                pe.wait_ge(sem("p_landed"), 16 * (l + 1))
                for k in range(2):
                    for t in range(TT):
                        mm = pe.transpose(B[4][:, k * SEQ + t * P:k * SEQ + (t + 1) * P], PIN[:, t, k * P:(k + 1) * P], ident)
                mm.then_inc(sem("pT_ready"), 1)
                pe.wait_ge(sem("pT_copied"), l + 1)
                s, v = landed(n)
                pe.wait_ge(s, v)
                wp = unit(n)[:, 0:2 * D].rearrange("p (k n) -> p k n", k=2)
                for t in range(TT):
                    for half in range(2):
                        pe.wait_ge(sem("h_updates"), 12 * l + 4 + 2 * t + half + 1)
                        for k in range(2):
                            mm = pe.matmul(B[2 * t + half][:, :], PINT[:, k, t * P:(t + 1) * P],
                                           wp[:, k, half * 512:(half + 1) * 512], start=(k == 0), stop=(k == 1))
                mm.then_inc(sem("pp_ready"), 1)
                pe.drain().then_inc(sem("units_used"), 1)
                transposes(3 * l + 2)
                xt_ready(3 * l + 2)
                project(n + 1, (4, 6), XT, done="pg_ready")
                project(n + 2, (5, 7), XT, done="pg_ready")

            experts(0, U_MOE0)
            ple(0, U_PLE0)

            transposes(3)
            xt_ready(3)

            def res_free(t):
                pe.wait_ge(sem("h_updates"), 12)
            project(U_QKV, (0, 1), XT, free=res_free, done="qkv_ready")
            project(U_QKV + 1, (2, 3), XT, done="qkv_ready")
            project(U_QKV + 2, (4, 5), XT, width=256, done="qkv_ready")
            for t in range(TT):
                pe.wait_ge(sem("q1_rotated"), t + 1)
                for c in range(8):
                    bank = (6, 7, 0, 1)[c // 2]
                    mm = pe.transpose(B[bank][:, (c % 2) * SEQ + t * P:(c % 2) * SEQ + (t + 1) * P],
                                      Q1[:, t, c * P:(c + 1) * P], ident)
                    if t == 1 and c % 2:
                        mm.then_inc(sem("q1_turned"), 1)
                for g in range(SKV):
                    mm = pe.transpose(B[2][:, g * SEQ + t * P:g * SEQ + (t + 1) * P],
                                      KDUP[:, t, g].rearrange("p r n -> p (r n)"), ident)
            mm.then_inc(sem("k1_turned"), 1)
            pe.wait_ge(sem("q1T_by_dve"), 2)
            pe.wait_ge(sem("q1T_by_act"), 2)
            pe.wait_ge(sem("k1T_copied"), 1)

            def odd_group(g):
                t, heads = odd_heads(g)
                return t, heads, (128, 192)[t]

            def scores1(g):
                t, heads, keys = odd_group(g)
                if g >= 2:
                    pe.wait_ge(sem("s1_scaled"), g - 1)
                for i, h in enumerate(heads):
                    r = 64 * (h % 2)
                    mm = pe.matmul(B[4 + g % 2][:, i * keys:(i + 1) * keys], Q1T[r:r + 64, h // 2, t * P:(t + 1) * P],
                                   K1T[r:r + 64, h // 8, 64 * t:64 * t + keys], start=True, stop=True)
                mm.then_inc(sem("s1_ready"), 1)

            def probs1(g):
                pe.wait_ge(sem("s1_exp"), sum(len(odd_group(n)[1]) for n in range(g + 1)))
                if g >= 2:
                    pe.wait_ge(sem("pt1_copied"), g - 1)
                for i in range(4):
                    mm = pe.transpose(B[6 + g % 2][:, i * P:(i + 1) * P], SC1[g % 2][:, i * P:(i + 1) * P], ident)
                mm.then_inc(sem("pt1_ready"), 1)

            def values1(g):
                t, heads, keys = odd_group(g)
                pe.wait_ge(sem("pt1_copied"), g + 1)
                kt = 1 + t
                for i, h in enumerate(heads):
                    for n in range(kt):
                        mm = pe.matmul(B[2 * t + h // 8][:, (h % 8) * HD:(h % 8 + 1) * HD],
                                       PT1[g % 2][:, (i * kt + n) * P:(i * kt + n + 1) * P],
                                       KV[:, n, 128 + (h // 8) * HD:128 + (h // 8 + 1) * HD],
                                       start=(n == 0), stop=(n == kt - 1))
                mm.then_inc(sem("pv1_ready"), 1)

            for g in range(12 + 2):
                if g < 12:
                    scores1(g)
                if 1 <= g <= 12:
                    probs1(g - 1)
                if g >= 2:
                    values1(g - 2)
            for t in range(TT):
                pe.wait_ge(sem("att1_out"), t + 1)
                for c in range(8):
                    mm = pe.transpose(B[4 + c // 2][:, (c % 2) * SEQ + t * P:(c % 2) * SEQ + (t + 1) * P],
                                      MIX1[:, t, c * P:(c + 1) * P], ident)
                    if t == 1 and c % 2:
                        mm.then_inc(sem("mix1_turned"), 1)
            pe.wait_ge(sem("mix1T_by_dve"), 2)
            pe.wait_ge(sem("mix1T_by_act"), 2)
            project(U_OUT1, (0, 1), XT, done="out1_ready")
            project(U_OUT1 + 1, (2, 3), XT, done="out1_ready")
            experts(1, U_MOE1)
            ple(1, U_PLE1)

        @block.scalar
        def _(act):
            def squares(k, src_ready):
                src_ready()
                for t in range(TT):
                    act.activation(HS[:, t, :], H[:, t, :], ACT.Square, accum_out=ST[:, t:t + 1])\
                        .then_inc(sem("squares_ready"), 1)

            def xt_evac(k):
                for q in (1, 3):
                    act.wait_ge(sem("hT_ready"), 4 * k + q + 1)
                    for kk in range(2):
                        i = act.activation(XT[:, 2 * q + kk, :], B[4 + q][:, kk * SEQ:(kk + 1) * SEQ], ACT.Copy,
                                           scale=NW[:, k, 2 * q + kk:2 * q + kk + 1])
                    i.then_inc(sem("xT_by_act"), 1)

            def copy(dst, src):
                return act.activation(dst, src, ACT.Copy)

            act.dma_start(DEC.rearrange("p h s -> p (h s)"), decay).then_inc(sem("decay_landed"), 16)
            act.dma_start(REL[:, 0:257], even_rel_bias[0]).then_inc(sem("rel_landed"), 16)
            act.wait_ge(sem("rel_reversed"), 2)
            act.dma_start(rel_rows, REL[:, 384:384 + REL_W]).then_inc(sem("rel_stored"), 16)
            act.wait_ge(sem("rel_stored"), 16)
            act.dma_start(FLIP, flip).then_inc(sem("bias_landed"), 16)
            act.dma_start(TOEP.rearrange("p (h s) -> p h s", h=CH), toeplitz(rel_rows)).then_inc(sem("bias_landed"), 16)

            squares(0, lambda: act.wait_ge(sem("x_landed"), 16))
            act.wait_ge(sem("small_landed"), 16 * 16)
            xt_evac(0)

            dst = {0: STG[0], 1: STG[1], 2: AV, 3: STG[0], 4: RVV}

            def in_evac(u):
                act.wait_ge(sem("in_ready"), 2 * u + 2)
                if u == 3:
                    act.wait_ge(sem("aqk_turned"), 2)
                copy(dst[u][:, 1, :], B[2 * (u % 2) + 1][:, :]).then_inc(sem("in_by_act"), 1)

            def even_heads(g):
                return (4, 128) if g < 2 else (2, 256)

            def exps0(g):
                nh, keys = even_heads(g)
                act.wait_ge(sem("max0_ready"), g + 1)
                for i in range(nh):
                    h = head0(g, i)
                    t = 0 if g < 2 else 1
                    s = SC0[g % 2][:, i * keys:(i + 1) * keys]
                    act.activation(s, s, ACT.Exp, bias=SM[:, t, h:h + 1], accum_out=SM[:, 2 + t, h:h + 1])\
                        .then_inc(sem("s0_exp"), 1)

            def pt_evac0(g):
                act.wait_ge(sem("pt0_ready"), g + 1)
                if g >= 2:
                    act.wait_ge(sem("pv0_ready"), g - 1)
                copy(PT0[g % 2][:, :], B[6][:, :]).then_inc(sem("pt0_copied"), 1)

            in_evac(0)
            in_evac(1)
            act.wait_ge(sem("aqk_turned"), 2)
            copy(AQT[:, 2:4, :].rearrange("p c s -> p (c s)"), B[5][:, :]).then_inc(sem("aqkT_by_act"), 1)
            act.wait_ge(sem("aqk_turned"), 4)
            copy(AKT[:, 2:4, :].rearrange("p c s -> p (c s)"), B[7][:, :]).then_inc(sem("aqkT_by_act"), 1)
            in_evac(2)
            exps0(0)
            exps0(1)
            in_evac(3)
            pt_evac0(0)
            pt_evac0(1)
            exps0(2)
            exps0(3)
            in_evac(4)
            pt_evac0(2)
            pt_evac0(3)
            exps0(4)
            exps0(5)
            for t in range(TT):
                act.wait_ge(sem("in_ready"), 10 + t + 1)
                act.activation(THR[:, t, :], B[2 + t][:, :], ACT.Tanh, scale=0.5).then_inc(sem("rg_tanh"), 1)
            pt_evac0(4)
            pt_evac0(5)
            act.wait_ge(sem("rqk_turned"), 2)
            copy(RT4[:, 2:4, :].rearrange("p c s -> p (c s)"), B[5][:, :]).then_inc(sem("rqkT_by_act"), 1)
            act.wait_ge(sem("mix0_turned"), 2)
            copy(XT[:, 6:8, :].rearrange("p c s -> p (c s)"), B[7][:, :]).then_inc(sem("mix0T_by_act"), 1)
            act.wait_ge(sem("mix0_turned"), 4)
            act.wait_ge(sem("gn_halved"), 1)
            for c in range(2):
                i = act.activation(XT[:, 2 + c, :], B[5][:, c * SEQ:(c + 1) * SEQ], ACT.Copy, scale=GN[:, 2 + c:3 + c])
            i.then_inc(sem("mix0T_by_act"), 1)

            def h_ready(n):
                return lambda: act.wait_ge(sem("h_updates"), 4 * n)

            def experts(l):
                k = 3 * l + 1
                squares(k, h_ready(3 * l + 1))
                xt_evac(k)
                act.wait_ge(sem("g_below_max"), l + 1)
                act.activation(RT[:, 20:28], RT[:, 20:28], ACT.Exp).then_inc(sem("g_exp"), 1)
                act.wait_ge(sem("second_below_first"), l + 1)
                act.activation(RT[:, 84:86], RT[:, 84:86], ACT.Exp).then_inc(sem("second_exp"), 1)
                act.wait_ge(sem("gates_turned"), l + 1)
                copy(GT[:, 2:4, :].rearrange("p s t -> p (s t)"), B[7][:, :]).then_inc(sem("gates_copied"), 1)
                act.wait_ge(sem("table_ready"), 2 * (l + 1))
                nb = act.value_load(TBL[0:1, 16:17], min_val=1, max_val=MAXB - 1)
                with act.Fori(0, nb) as b:
                    off = act.value_load(TBL[0:1, bass.ds(b + 17, 1)], min_val=0, max_val=SLOTS)
                    act.wait_ge(sem(f"gu{l}_ready"), b * 2 + 1)
                    act.activation(TH, B[2][:, 0:256], ACT.Tanh, scale=0.5).then_inc(sem(f"th{l}_ready"), 1)
                    act.wait_ge(sem(f"y{l}_ready"), b + 1)
                    act.activation(YT[:, :, bass.ds(off, BLK)], B[5][:, :].rearrange("p (k s) -> p k s", k=KD), ACT.Copy)\
                        .then_inc(sem(f"y{l}_free"), 1)
                for s in range(4):
                    act.wait_ge(sem("ys_ready"), 8 * l + 2 * s + 2)
                    copy(YS[:, s, 512:1024], B[4 + (2 * s + 1) % 4][:, :]).then_inc(sem("ys_by_act"), 1)

            def ple(l):
                act.wait_ge(sem("h_updates"), 12 * l + 8)
                act.dma_start(PIN, p[l, 0].rearrange("(t p) d -> p t d", p=P)).then_inc(sem("p_landed"), 16)
                if l == 1:
                    act.dma_start(FW, bcast(final_norm.rearrange("(a d) -> a d", a=1))).then_inc(sem("fw_landed"), 16)
                squares(3 * l + 2, h_ready(3 * l + 2))
                act.wait_ge(sem("pT_ready"), l + 1)
                copy(PINT.rearrange("p k s -> p (k s)"), B[4][:, :]).then_inc(sem("pT_copied"), 1)
                xt_evac(3 * l + 2)
                for half in range(2):
                    for t in range(TT):
                        act.wait_ge(sem("pg_ready"), 4 * l + 2 * half + t + 1)
                        act.activation(THG[:, t, half * 512:(half + 1) * 512], B[4 + half + 2 * t][:, :], ACT.Tanh,
                                       scale=0.5).then_inc(sem("pg_tanh"), 1)

            experts(0)
            ple(0)

            act.wait_ge(sem("h_updates"), 12)
            act.dma_start(BQ, bcast(odd_b_qkv)).then_inc(sem("bq_landed"), 16)
            squares(3, h_ready(3))
            xt_evac(3)
            act.wait_ge(sem("q1_turned"), 2)
            copy(Q1T[:, 2:4, :].rearrange("p c s -> p (c s)"), B[7][:, :]).then_inc(sem("q1T_by_act"), 1)
            act.wait_ge(sem("q1_turned"), 4)
            copy(Q1T[:, 6:8, :].rearrange("p c s -> p (c s)"), B[1][:, :]).then_inc(sem("q1T_by_act"), 1)
            act.dma_start(BO, bcast(odd_b_out)).then_inc(sem("bo_landed"), 16)

            def exps1(g):
                act.wait_ge(sem("max1_ready"), g + 1)
                t, heads = odd_heads(g)
                for i, h in enumerate(heads):
                    s = SC1[g % 2][:, i * 128:(i + 1) * 128] if t == 0 else SC1[g % 2][:, i * 256 + 64:(i + 1) * 256]
                    act.activation(s, s, ACT.Exp, bias=SM[:, t, h:h + 1], accum_out=SM[:, 2 + t, h:h + 1])\
                        .then_inc(sem("s1_exp"), 1)

            def pt_evac1(g):
                act.wait_ge(sem("pt1_ready"), g + 1)
                if g >= 2:
                    act.wait_ge(sem("pv1_ready"), g - 1)
                copy(PT1[g % 2][:, :], B[6 + g % 2][:, :]).then_inc(sem("pt1_copied"), 1)

            for g in range(13):
                if g < 12:
                    exps1(g)
                if g >= 1:
                    pt_evac1(g - 1)
            for t in range(TT):
                act.wait_ge(sem("sink_below_max"), t + 1)
                act.activation(ES[:, t, :], ES[:, t, :], ACT.Exp).then_inc(sem("sink_exp"), 1)
            for q in (1, 3):
                act.wait_ge(sem("mix1_turned"), q + 1)
                copy(XT[:, 2 * q:2 * q + 2, :].rearrange("p c s -> p (c s)"), B[4 + q][:, :])\
                    .then_inc(sem("mix1T_by_act"), 1)
            experts(1)
            ple(1)
            squares(6, h_ready(6))

        @block.vector
        def _(dve):
            steps = [0]

            def then(ins):
                steps[0] += 1
                ins.then_inc(sem("dve_steps"), 1)
                dve.wait_ge(sem("dve_steps"), steps[0])

            def norm(k):
                dve.wait_ge(sem("squares_ready"), 2 * (k + 1))
                dve.tensor_scalar(ST[:, 2:4], ST[:, 0:2], 1.0 / D, EPS, ALU.mult, ALU.add).then_inc(sem("ms_ready"), 1)
                dve.wait_ge(sem("rstd_ready"), k + 1)
                for t in range(TT):
                    if k < 6:
                        dve.tensor_scalar(HS[:, t, :], H[:, t, :], ST[:, 4 + t:5 + t], None, ALU.mult)\
                            .then_inc(sem("hs_ready"), 1)

            def xt_evac(k):
                for q in (0, 2):
                    dve.wait_ge(sem("hT_ready"), 4 * k + q + 1)
                    dve.tensor_tensor(XT[:, 2 * q:2 * q + 2, :], B[4 + q][:, :].rearrange("p (k s) -> p k s", k=2),
                                      NW[:, k, 2 * q:2 * q + 2].unsqueeze(2).to_broadcast([P, 2, SEQ]), ALU.mult)\
                        .then_inc(sem("xT_by_dve"), 1)

            dve.wait_ge(sem("rel_landed"), 16)
            dve.tensor_copy(REL[:, 384 + 127:384 + REL_W], REL[:, 256:0:-1]).then_inc(sem("rel_reversed"), 1)
            dve.tensor_copy(REL[:, 384:384 + 127], REL[:, 256:257].to_broadcast([CH, 127])).then_inc(sem("rel_reversed"), 1)
            norm(0)
            dve.wait_ge(sem("small_landed"), 16 * 16)
            xt_evac(0)
            dve.tensor_scalar(GN[:, :], GN[:, :], 0.5, None, ALU.mult).then_inc(sem("gn_halved"), 1)

            dst = {0: STG[0], 1: STG[1], 2: AV, 3: STG[0], 4: RVV}

            def in_evac(u):
                dve.wait_ge(sem("in_ready"), 2 * u + 1)
                if u == 3:
                    dve.wait_ge(sem("aqk_turned"), 2)
                dve.tensor_copy(dst[u][:, 0, :], B[2 * (u % 2)][:, :]).then_inc(sem("in_by_dve"), 1)

            def scale0(g):
                t = 0 if g < 2 else 1
                nh, keys = (4, 128) if t == 0 else (2, 256)
                h0 = head0(g, 0)
                dve.wait_ge(sem("s0_ready"), g + 1)
                if g >= 2:
                    dve.wait_ge(sem("pt0_ready"), g - 1)
                sc = SC0[g % 2].rearrange("p (h s) -> p h s", h=nh)
                dve.scalar_tensor_tensor(out=sc, in0=B[4 + g % 2][:, :].rearrange("p (h s) -> p h s", h=nh),
                                         scalar=HD ** -0.5, in1=BIAS[:, h0:h0 + 2 * nh - 1:2, 256 - keys:256],
                                         op0=ALU.mult, op1=ALU.add).then_inc(sem("s0_scaled"), 1)
                dve.wait_ge(sem("s0_scaled"), g + 1)
                dve.tensor_reduce(SM[:, t, h0:h0 + 2 * nh - 1:2], sc, AX.X, ALU.max, negate=True)\
                    .then_inc(sem("max0_ready"), 1)

            def att_out0(t):
                dve.wait_ge(sem("s0_exp"), 8 * (t + 1))
                then(dve.reciprocal(SM[:, 2 + t, 0:CH], SM[:, 2 + t, 0:CH]))
                dve.wait_ge(sem("pv0_ready"), 2 + 4 * t)
                dve.tensor_tensor(MIXA[:, t, :].rearrange("p (h n) -> p h n", h=CH),
                                  B[7][:, :].rearrange("p (h n) -> p h n", h=CH),
                                  SM[:, 2 + t, 0:CH].unsqueeze(2).to_broadcast([P, CH, HD]), ALU.mult)\
                    .then_inc(sem("att0_out"), 1)

            in_evac(0)
            for n in range(4):
                dve.wait_ge(sem("bias_ready"), n + 1)
                src = B[4 + n][:, :].rearrange("p (h s) -> p h s", h=2)
                dve.tensor_copy(BIAS[:, 2 * n:2 * n + 2, 0:128], src[:, :, 0:128])
                dve.tensor_tensor(BIAS[:, 2 * n:2 * n + 2, 128:256], src[:, :, 128:256],
                                  C[:, C_M0:C_M0 + P].unsqueeze(1).to_broadcast([P, 2, P]), ALU.add)\
                    .then_inc(sem("bias_copied"), 1)
            in_evac(1)
            dve.wait_ge(sem("aqk_turned"), 1)
            dve.tensor_copy(AQT[:, 0:2, :].rearrange("p c s -> p (c s)"), B[4][:, :]).then_inc(sem("aqkT_by_dve"), 1)
            dve.wait_ge(sem("aqk_turned"), 3)
            dve.tensor_copy(AKT[:, 0:2, :].rearrange("p c s -> p (c s)"), B[6][:, :]).then_inc(sem("aqkT_by_dve"), 1)
            in_evac(2)
            dve.wait_ge(sem("bias_copied"), 4)
            scale0(0)
            scale0(1)
            in_evac(3)
            scale0(2)
            scale0(3)
            att_out0(0)

            def rotate(t):
                cosr = C[:, C_COSR + 64 * t:C_COSR + 64 * t + 64].unsqueeze(1).to_broadcast([P, 8, 64])
                sinr = C[:, C_SINR + 64 * t:C_SINR + 64 * t + 64]
                raw = STG[0][:, t, :].rearrange("p (h n) -> p h n", h=8)
                tmp = RTB[:, t, :].rearrange("p (h n) -> p h n", h=8)
                o = RRO[:, t, :].rearrange("p (h n) -> p h n", h=8)
                dve.tensor_tensor(o, raw, cosr, ALU.mult)
                dve.tensor_tensor(tmp[:, :, 0:32], raw[:, :, 32:64], sinr[:, 0:32].unsqueeze(1).to_broadcast([P, 8, 32]),
                                  ALU.mult)
                then(dve.tensor_tensor(tmp[:, :, 32:64], raw[:, :, 0:32],
                                       sinr[:, 32:64].unsqueeze(1).to_broadcast([P, 8, 32]), ALU.mult))
                dve.tensor_tensor(o, o, tmp, ALU.add).then_inc(sem("ret_rotated"), 1)

            dve.wait_ge(sem("in_by_act"), 4)
            dve.wait_ge(sem("in_by_dve"), 4)
            rotate(0)
            rotate(1)
            in_evac(4)
            scale0(4)
            scale0(5)
            for t in range(TT):
                dve.wait_ge(sem("rg_tanh"), t + 1)
                dve.scalar_tensor_tensor(out=GATE[:, t, :], in0=THR[:, t, :], scalar=1.0, in1=B[2 + t][:, :],
                                         op0=ALU.add, op1=ALU.mult).then_inc(sem("gate_ready"), 1)
            att_out0(1)
            dve.wait_ge(sem("rqk_turned"), 1)
            dve.tensor_copy(RT4[:, 0:2, :].rearrange("p c s -> p (c s)"), B[4][:, :]).then_inc(sem("rqkT_by_dve"), 1)
            for par in range(2):
                dve.wait_ge(sem("rs_ready"), par + 1)
                dve.tensor_tensor(RP0[:, 2 * par:2 * par + 2, :], B[4 + par][:, :].rearrange("p (h s) -> p h s", h=2),
                                  DEC[:, 2 * par:2 * par + 2, :], ALU.mult).then_inc(sem("rs_decayed"), 1)
            for par in range(2):
                dve.wait_ge(sem("rs_ready"), par + 3)
                dve.tensor_tensor(RP1[:, 2 * par:2 * par + 2, :], B[6 + par][:, 0:256].rearrange("p (h s) -> p h s", h=2),
                                  DEC[:, 2 * par:2 * par + 2, 0:P], ALU.mult).then_inc(sem("rs_decayed"), 1)
            for t in range(TT):
                dve.wait_ge(sem("ro_ready"), t + 1)
                for h in range(RH):
                    i = dve.bn_stats(BNS[:, t, h, :], B[t][:, h * RV:(h + 1) * RV])
            then(i)
            for t in range(TT):
                for h in range(RH):
                    i = dve.bn_aggr(BNA[:, t, h, :], BNS[:, t, h, :])
            then(i)
            dve.tensor_scalar(BNE.rearrange("p (t h) -> p t h", t=TT), BNA[:, :, :, 1], EPS, None, ALU.add)\
                .then_inc(sem("gn_ready"), 1)
            dve.wait_ge(sem("gn_rstd"), 1)
            for t in range(TT):
                for h in range(RH):
                    c = slice(h * RV, (h + 1) * RV)
                    i = dve.tensor_scalar(RET[:, t, c], B[t][:, c], BNA[:, t, h, 0:1], BNR[:, 4 * t + h:4 * t + h + 1],
                                          ALU.subtract, ALU.mult)
                then(i)
                dve.tensor_tensor(RET[:, t, :], RET[:, t, :], GATE[:, t, :], ALU.mult).then_inc(sem("ret_out"), 1)
            dve.wait_ge(sem("ret_out"), 2)
            dve.wait_ge(sem("mix0_turned"), 1)
            dve.tensor_copy(XT[:, 4:6, :].rearrange("p c s -> p (c s)"), B[6][:, :]).then_inc(sem("mix0T_by_dve"), 1)
            dve.wait_ge(sem("mix0_turned"), 3)
            dve.wait_ge(sem("gn_halved"), 1)
            dve.tensor_tensor(XT[:, 0:2, :], B[4][:, :].rearrange("p (k s) -> p k s", k=2),
                              GN[:, 0:2].unsqueeze(2).to_broadcast([P, 2, SEQ]), ALU.mult).then_inc(sem("mix0T_by_dve"), 1)
            for half in range(2):
                for t in range(TT):
                    dve.wait_ge(sem("out0_ready"), 2 * half + t + 1)
                    hh = H[:, t, half * 512:(half + 1) * 512]
                    dve.tensor_tensor(hh, hh, B[2 * half + t][:, :], ALU.add).then_inc(sem("h_updates"), 1)

            def experts(l):
                k = 3 * l + 1
                norm(k)
                xt_evac(k)
                t3 = lambda a, n: RT[:, a:a + 2 * n].rearrange("p (t n) -> p t n", t=TT)
                wide = lambda ap, n: ap.to_broadcast([P, TT, n])
                LG, LE = t3(140, 4), t3(148, 16)
                GB, GE, GX, GS, GOH = t3(20, 4), t3(28, 4), t3(36, 1), t3(38, 1), t3(40, 4)
                ES4, M1, EQ, MX, OH1 = t3(48, 4), t3(56, 1), t3(58, 4), t3(66, 1), t3(68, 4)
                OH2, SEC, W1, W2 = t3(76, 4), t3(84, 1), t3(86, 1), t3(88, 1)
                M2, GWT = t3(90, 1), t3(92, 1)
                M = t3(100, NE)
                O1, O2, EL, SLT = t3(180, NE), t3(212, NE), t3(244, NE), t3(276, NE)
                CNT, NBK, CI, NI, OFF, DEL = (RT[:, 308 + 16 * n:324 + 16 * n] for n in range(6))
                S1, S2 = t3(404, 1), t3(406, 1)
                rev = C[:, C_REV:C_REV + 4].unsqueeze(1).to_broadcast([P, TT, 4])
                dve.wait_ge(sem("logits_ready"), l + 1)
                lg = B[0][:, 0:40].rearrange("p (t n) -> p t n", t=TT)
                dve.tensor_tensor(LG, lg[:, :, 0:4], BR[:, l, 0:4].unsqueeze(1).to_broadcast([P, TT, 4]), ALU.add)
                then(dve.tensor_tensor(LE, lg[:, :, 4:20], BR[:, l, 4:20].unsqueeze(1).to_broadcast([P, TT, 16]), ALU.add))

                def first_max(val, mx, hot):
                    then(dve.tensor_reduce(mx, val, AX.X, ALU.max))
                    then(dve.tensor_tensor(EQ, val, wide(mx, 4), ALU.is_ge))
                    then(dve.tensor_tensor(EQ, EQ, rev, ALU.mult))
                    then(dve.tensor_reduce(MX, EQ, AX.X, ALU.max))
                    then(dve.tensor_tensor(hot, EQ, wide(MX, 4), ALU.is_equal))

                first_max(LG, GX, GOH)
                dve.tensor_tensor(GB, LG, wide(GX, 4), ALU.subtract).then_inc(sem("g_below_max"), 1)
                then(dve.tensor_tensor(EL.rearrange("p t (g e) -> p t g e", g=G), LE.rearrange("p t (g e) -> p t g e", g=G),
                                       GOH.unsqueeze(3).to_broadcast([P, TT, G, E]), ALU.mult))
                then(dve.tensor_reduce(ES4, EL.rearrange("p t (g e) -> p t e g", g=G), AX.X, ALU.add))
                first_max(ES4, M1, OH1)
                then(dve.scalar_tensor_tensor(out=ES4, in0=OH1, scalar=NEG, in1=ES4, op0=ALU.mult, op1=ALU.add))
                first_max(ES4, M2, OH2)
                dve.tensor_tensor(SEC, M2, M1, ALU.subtract).then_inc(sem("second_below_first"), 1)
                for oh, o in ((OH1, O1), (OH2, O2)):
                    for t in range(TT):
                        i = dve.tensor_tensor(o[:, t, :].rearrange("p (g e) -> p g e", g=G),
                                              GOH[:, t, :].unsqueeze(2).to_broadcast([P, G, E]),
                                              oh[:, t, :].unsqueeze(1).to_broadcast([P, G, E]), ALU.mult)
                then(i)
                dve.tensor_tensor(M, O1, O2, ALU.add).then_inc(sem("chosen"), 1)
                dve.wait_ge(sem("g_exp"), l + 1)
                then(dve.tensor_reduce(GS, GB, AX.X, ALU.add))
                then(dve.reciprocal(GWT, GS))
                dve.wait_ge(sem("second_exp"), l + 1)
                then(dve.tensor_scalar(W1, SEC, 1.0, None, ALU.add))
                then(dve.reciprocal(W1, W1))
                then(dve.tensor_tensor(W1, W1, GWT, ALU.mult))
                then(dve.tensor_tensor(W2, W1, SEC, ALU.mult))
                dve.wait_ge(sem("ranks_ready"), l + 1)
                then(dve.tensor_copy(CNT, B[1][:, 32:48]))
                then(dve.tensor_scalar(NBK, CNT, float(BLK), 1.0, ALU.is_gt, ALU.add))
                for n in range(2, SEQ // BLK):
                    then(dve.scalar_tensor_tensor(out=NBK, in0=CNT, scalar=float(n * BLK), in1=NBK,
                                                  op0=ALU.is_gt, op1=ALU.add))
                ones = C[:, C_ONE:C_ONE + NE]
                dve.tensor_tensor_scan(CI, ones, CNT, 0.0, ALU.mult, ALU.add)
                then(dve.tensor_tensor_scan(NI, ones, NBK, 0.0, ALU.mult, ALU.add))
                dve.tensor_tensor(OFF, CI, CNT, ALU.subtract)
                then(dve.tensor_tensor(NBK, NI, NBK, ALU.subtract))
                then(dve.scalar_tensor_tensor(out=DEL, in0=NBK, scalar=-float(BLK), in1=OFF, op0=ALU.mult, op1=ALU.add))
                then(dve.tensor_tensor(SLT, B[1][:, 0:32].rearrange("p (t e) -> p t e", t=TT),
                                       OFF.unsqueeze(1).to_broadcast([P, TT, NE]), ALU.add))
                for o, s in ((O1, S1), (O2, S2)):
                    then(dve.tensor_tensor(o, o, SLT, ALU.mult))
                    then(dve.tensor_reduce(s, o, AX.X, ALU.add))
                dve.wait_ge(sem("iota_ready"), 2 * l + 2)
                for t in range(TT):
                    dve.tensor_scalar(TMP[:, t, :], IOTA, S2[:, t, :], None, ALU.is_equal)
                    then(dve.tensor_scalar(GM[:, t, :], IOTA, S2[:, t, :], W2[:, t, :], ALU.is_equal, ALU.mult))
                    then(dve.scalar_tensor_tensor(out=PH[:, t, :], in0=IOTA, scalar=S1[:, t, :], in1=TMP[:, t, :],
                                                  op0=ALU.is_equal, op1=ALU.add))
                one = slice(0, 1)
                g3 = [g[one].rearrange("p (b e) -> p b e", b=MAXB) for g in GRID]
                wide_e = lambda a: a[one].unsqueeze(1).to_broadcast([1, MAXB, NE])
                dve.memset(TBL[0:1, 0:1], 0)
                dve.tensor_copy(TBL[0:1, 1:17], NI[one]).then_inc(sem("table_ready"), 1)
                dve.tensor_tensor(g3[1], g3[0], wide_e(NBK), ALU.is_ge)
                then(dve.tensor_tensor(g3[2], g3[0], wide_e(NI), ALU.is_lt))
                then(dve.tensor_tensor(g3[1], g3[1], g3[2], ALU.mult))
                then(dve.scalar_tensor_tensor(out=g3[2], in0=g3[0], scalar=float(BLK), in1=wide_e(DEL),
                                              op0=ALU.mult, op1=ALU.add))
                then(dve.tensor_tensor(g3[1], g3[1], g3[2], ALU.mult))
                then(dve.tensor_reduce(RT[one, 100:132], g3[1], AX.X, ALU.add))
                dve.tensor_copy(TBL[0:1, 17:17 + MAXB], RT[one, 100:132]).then_inc(sem("table_ready"), 1)
                dve.wait_ge(sem("table_ready"), 2 * (l + 1))

                dve.tensor_copy(PBLK, PH[:, :, 0:BLK]).then_inc(sem(f"pblk{l}_ready"), 1)
                for t in range(TT):
                    then(dve.tensor_scalar(TMP[:, t, :], IOTA, S1[:, t, :], W1[:, t, :], ALU.is_equal, ALU.mult))
                    i = dve.tensor_tensor(GM[:, t, :], GM[:, t, :], TMP[:, t, :], ALU.add)
                i.then_inc(sem("gates_ready"), 1)
                nwb = NW[:, k, :].unsqueeze(2).to_broadcast([P, KD, BLK])
                rows = B[4][:, :].rearrange("p (k s) -> p k s", k=KD)
                dve.wait_ge(sem(f"rows{l}_ready"), 1)
                dve.tensor_tensor(XBLK, rows, nwb, ALU.mult).then_inc(sem(f"xblk{l}_ready"), 1)
                dve.wait_ge(sem("gates_turned"), l + 1)
                dve.tensor_copy(GT[:, 0:2, :].rearrange("p s t -> p (s t)"), B[6][:, :]).then_inc(sem("gates_copied"), 1)
                nb = dve.value_load(TBL[0:1, 16:17], min_val=1, max_val=MAXB - 1)
                dve.wait_ge(sem("gates_copied"), 2 * l + 2)
                dve.memset(AG, 0.0).then_inc(sem(f"y{l}_free"), 1)
                dve.wait_ge(sem(f"y{l}_free"), 1)
                with dve.Fori(0, nb) as b:
                    off = dve.value_load(TBL[0:1, bass.ds(b + 18, 1)], min_val=0, max_val=SLOTS)
                    dve.wait_ge(sem(f"rows{l}_ready"), b + 1)
                    dve.tensor_copy(PBLK, PH[:, :, bass.ds(off, BLK)]).then_inc(sem(f"pblk{l}_ready"), 1)
                    dve.wait_ge(sem(f"th{l}_ready"), b + 1)
                    dve.scalar_tensor_tensor(out=AG, in0=TH, scalar=1.0, in1=B[2][:, 0:256], op0=ALU.add,
                                             op1=ALU.mult).then_inc(sem(f"ag{l}_ready"), 1)
                    dve.wait_ge(sem(f"ag{l}_ready"), b + 1)
                    dve.wait_ge(sem(f"gu{l}_ready"), b * 2 + 2)
                    dve.scalar_tensor_tensor(out=ACTT, in0=AG, scalar=0.5, in1=B[3][:, 0:256], op0=ALU.mult,
                                             op1=ALU.mult).then_inc(sem(f"act{l}_ready"), 1)
                    dve.wait_ge(sem(f"rows{l}_ready"), b + 2)
                    dve.tensor_tensor(XBLK, rows, nwb, ALU.mult).then_inc(sem(f"xblk{l}_ready"), 1)
                for s in range(4):
                    dve.wait_ge(sem("ys_ready"), 8 * l + 2 * s + 1)
                    dve.tensor_copy(YS[:, s, 0:512], B[4 + (2 * s) % 4][:, :]).then_inc(sem("ys_by_dve"), 1)
                for t in range(TT):
                    for half in range(2):
                        dve.wait_ge(sem("moe_ready"), 4 * l + 2 * t + half + 1)
                        hh = H[:, t, half * 512:(half + 1) * 512]
                        dve.tensor_tensor(hh, hh, B[2 * t + half][:, :], ALU.add).then_inc(sem("h_updates"), 1)

            def ple(l):
                norm(3 * l + 2)
                xt_evac(3 * l + 2)
                dve.wait_ge(sem("pp_ready"), l + 1)
                for half in range(2):
                    for t in range(TT):
                        dve.wait_ge(sem("pg_tanh"), 4 * l + 2 * half + t + 1)
                        c = slice(half * 512, (half + 1) * 512)
                        then(dve.scalar_tensor_tensor(out=THG[:, t, c], in0=THG[:, t, c], scalar=1.0,
                                                      in1=B[2 * t + half][:, :], op0=ALU.add, op1=ALU.mult))
                        dve.scalar_tensor_tensor(out=H[:, t, c], in0=THG[:, t, c], scalar=0.5, in1=H[:, t, c],
                                                 op0=ALU.mult, op1=ALU.add).then_inc(sem("h_updates"), 1)

            experts(0)
            ple(0)

            norm(3)
            xt_evac(3)
            dve.wait_ge(sem("bq_landed"), 16)
            for u in range(2):
                for t in range(TT):
                    dve.wait_ge(sem("qkv_ready"), 2 * u + t + 1)
                    dve.tensor_tensor(Q1[:, t, 512 * u:512 * u + 512], B[2 * u + t][:, :], BQ[:, 512 * u:512 * u + 512],
                                      ALU.add)
            for t in range(TT):
                dve.wait_ge(sem("qkv_ready"), 4 + t + 1)
                then(dve.tensor_tensor(KV[:, t, :], B[4 + t][:, 0:256], BQ[:, 1024:1280], ALU.add))
            for t in range(TT):
                for a, n, h0 in ((Q1[:, t, :], SH, 0), (KV[:, t, 0:128], SKV, SH)):
                    v = a.rearrange("p (h n) -> p h n", h=n)
                    cs = C[:, C_COSO + ROT * t:C_COSO + ROT * (t + 1)].unsqueeze(1).to_broadcast([P, n, ROT])
                    si = C[:, C_SINO + ROT * t:C_SINO + ROT * (t + 1)]
                    tmp = RB1[:, t, h0:h0 + n, :]
                    dve.tensor_tensor(tmp[:, :, 0:8], v[:, :, 8:16], si[:, 0:8].unsqueeze(1).to_broadcast([P, n, 8]), ALU.mult)
                    then(dve.tensor_tensor(tmp[:, :, 8:16], v[:, :, 0:8],
                                           si[:, 8:16].unsqueeze(1).to_broadcast([P, n, 8]), ALU.mult))
                    then(dve.tensor_tensor(v[:, :, 0:ROT], v[:, :, 0:ROT], cs, ALU.mult))
                    then(dve.tensor_tensor(v[:, :, 0:ROT], v[:, :, 0:ROT], tmp, ALU.add))
                dve.tensor_copy(KDUP[:, t, :, 0, :], KV[:, t, 0:128].rearrange("p (g n) -> p g n", g=SKV))
                dve.tensor_copy(KDUP[:, t, :, 1, :], KV[:, t, 0:128].rearrange("p (g n) -> p g n", g=SKV))\
                    .then_inc(sem("q1_rotated"), 1)
            dve.wait_ge(sem("q1_turned"), 1)
            dve.tensor_copy(Q1T[:, 0:2, :].rearrange("p c s -> p (c s)"), B[6][:, :]).then_inc(sem("q1T_by_dve"), 1)
            dve.wait_ge(sem("q1_turned"), 3)
            dve.tensor_copy(Q1T[:, 4:6, :].rearrange("p c s -> p (c s)"), B[0][:, :]).then_inc(sem("q1T_by_dve"), 1)
            dve.wait_ge(sem("k1_turned"), 1)
            dve.tensor_copy(K1T.rearrange("p g s -> p (g s)"), B[2][:, :]).then_inc(sem("k1T_copied"), 1)

            def scale1(g):
                t, heads = odd_heads(g)
                nh, keys, h0 = len(heads), (128, 192)[t], heads[0]
                dve.wait_ge(sem("s1_ready"), g + 1)
                if g >= 2:
                    dve.wait_ge(sem("pt1_ready"), g - 1)
                if t == 0:
                    sc = SC1[g % 2].rearrange("p (h s) -> p h s", h=nh)
                else:
                    full = SC1[g % 2].rearrange("p (h s) -> p h s", h=nh)
                    sc = full[:, :, 64:256]
                    if g < 6:
                        dve.memset(full[:, :, 0:64], 0.0)
                mask = C[:, C_M0:C_M0 + P] if t == 0 else C[:, C_M1:C_M1 + 192]
                dve.scalar_tensor_tensor(out=sc, in0=B[4 + g % 2][:, 0:nh * keys].rearrange("p (h s) -> p h s", h=nh),
                                         scalar=HD ** -0.5, in1=mask.unsqueeze(1).to_broadcast([P, nh, keys]),
                                         op0=ALU.mult, op1=ALU.add).then_inc(sem("s1_scaled"), 1)
                dve.wait_ge(sem("s1_scaled"), g + 1)
                hs = slice(h0, h0 + 2 * nh - 1, 2)
                then(dve.tensor_reduce(SM[:, t, hs], sc, AX.X, ALU.max))
                then(dve.tensor_tensor(SM[:, t, hs], SM[:, t, hs], SK[:, hs], ALU.max))
                dve.tensor_scalar(SM[:, t, hs], SM[:, t, hs], -1.0, None, ALU.mult).then_inc(sem("max1_ready"), 1)

            def att_out1(t):
                dve.wait_ge(sem("max1_ready"), (4, 12)[t])
                dve.tensor_tensor(ES[:, t, :], SM[:, t, :], SK[:, :], ALU.add).then_inc(sem("sink_below_max"), 1)
                dve.wait_ge(sem("sink_exp"), t + 1)
                dve.wait_ge(sem("s1_exp"), SH * (t + 1))
                then(dve.tensor_tensor(SM[:, 2 + t, :], SM[:, 2 + t, :], ES[:, t, :], ALU.add))
                then(dve.reciprocal(SM[:, 2 + t, :], SM[:, 2 + t, :]))
                dve.wait_ge(sem("pv1_ready"), (4, 12)[t])
                for n in range(2):
                    i = dve.tensor_tensor(MIX1[:, t, 512 * n:512 * n + 512].rearrange("p (h n) -> p h n", h=8),
                                          B[2 * t + n][:, :].rearrange("p (h n) -> p h n", h=8),
                                          SM[:, 2 + t, 8 * n:8 * n + 8].unsqueeze(2).to_broadcast([P, 8, HD]), ALU.mult)
                i.then_inc(sem("att1_out"), 1)

            for g in range(12):
                scale1(g)
            dve.wait_ge(sem("bo_landed"), 16)
            for t in range(TT):
                then(dve.tensor_tensor(H[:, t, :], H[:, t, :], BO, ALU.add))
            att_out1(0)
            att_out1(1)
            for q in (0, 2):
                dve.wait_ge(sem("mix1_turned"), q + 1)
                dve.tensor_copy(XT[:, 2 * q:2 * q + 2, :].rearrange("p c s -> p (c s)"), B[4 + q][:, :])\
                    .then_inc(sem("mix1T_by_dve"), 1)
            for half in range(2):
                for t in range(TT):
                    dve.wait_ge(sem("out1_ready"), 2 * half + t + 1)
                    hh = H[:, t, half * 512:(half + 1) * 512]
                    dve.tensor_tensor(hh, hh, B[2 * half + t][:, :], ALU.add).then_inc(sem("h_updates"), 1)
            experts(1)
            ple(1)
            norm(6)
            dve.wait_ge(sem("fw_landed"), 16)
            for t in range(TT):
                dve.scalar_tensor_tensor(out=OUTB[:, t, :], in0=H[:, t, :], scalar=ST[:, 4 + t:5 + t], in1=FW,
                                         op0=ALU.mult, op1=ALU.mult).then_inc(sem("out_ready"), 1)


_INS = ["x", "p", "norm_mix", "norm_ffn", "norm_ple", "final_norm", "even_w_in", "even_ret_gn", "even_rel_bias",
        "even_w_out", "odd_w_qkv", "odd_b_qkv", "odd_sinks", "odd_w_out", "odd_b_out", "moe_w_group", "moe_b_group",
        "moe_w_router", "moe_b_router", "moe_w_gate", "moe_w_up", "moe_w_down", "ple_w_proj", "ple_w_gate"]


def kernel(**inputs):
    import concourse.bacc as bacc
    from concourse.bass_utils import run_bass_kernel_spmd

    nc = bacc.Bacc("TRN2", target_bir_lowering=False, num_devices=1)
    const, decay = constants()
    flip = np.ascontiguousarray(np.eye(P, dtype=np.float32)[::-1])
    arrays, args = {}, []
    for name, a in [(n, inputs[n]) for n in _INS] + [("const", const), ("decay", decay), ("flip", flip)]:
        a = np.ascontiguousarray(a)
        arrays[f"in_{name}_dram"] = a
        args.append(nc.dram_tensor(f"in_{name}_dram", a.shape, mybir.dt.from_np(a.dtype), kind="ExternalInput").ap())
    args.append(nc.dram_tensor("out_0_dram", (1, SEQ, D), F32, kind="ExternalOutput").ap())
    args.append(nc.dram_tensor("rel_rows_dram", (CH, REL_W), F32, kind="Internal").ap())
    build(nc, *args)
    r = run_bass_kernel_spmd(nc, [arrays], core_ids=[0])
    return r.results[0]["out_0_dram"]
```

```python
from contextlib import ExitStack

import numpy as np

import concourse.bass as bass
from concourse import mybir

F32 = mybir.dt.float32
F32R = mybir.dt.float32r
I32 = mybir.dt.int32
ALU = mybir.AluOpType
ACT = mybir.ActivationFunctionType
AX = mybir.AxisListType

P = 128
D = 1024
KD = D // P
SEQ = 256
TT = SEQ // P
EPS = 1e-6
NEG = -1e30
CHUNK = 64

RH, RV = 4, 128
CH = 8
HD = 64
SH, SKV = 16, 2
ROT = 16
MAXREL = 128
REL_W = 3 * P - 1
G, E = 4, 4
NE = G * E
FF = 512
KF = FF // P
PD = 256

BLK = 64
SLOTS = 2 * SEQ
LAST = SLOTS - BLK
MAXOV = 8

NSLOT = 6
NCH = 4
UN = 4096

U_IN, U_OUT0 = 0, 6
U_MOE0 = 8
U_PLE0 = U_MOE0 + 3 * NE
U_QKV, U_OUT1 = U_PLE0 + 3, U_PLE0 + 6
U_MOE1 = U_OUT1 + 2
U_PLE1 = U_MOE1 + 3 * NE

C_ID, C_LOW, C_ONE, C_M0, C_M1 = 0, 128, 256, 384, 512
C_COSR, C_SINR, C_COSO, C_SINO, C_REV, C_PM = 704, 832, 960, 992, 1024, 1028
C_N = 1029


def constants():
    c = np.zeros((P, C_N), np.float32)
    i = np.arange(P)
    c[:, C_ID:C_ID + P] = np.eye(P)
    c[:, C_LOW:C_LOW + P] = i[:, None] < i[None, :]
    c[:, C_ONE:C_ONE + P] = 1.0
    first = i < CHUNK
    c[:, C_M0:C_M0 + P] = np.where(first[:, None] & ~first[None, :], NEG, 0.0)
    j = np.arange(192)
    c[:, C_M1:C_M1 + 192] = np.where(first[:, None], (j >= 128)[None, :], (j < 64)[None, :]) * np.float32(NEG)

    def rotary(dim, theta):
        half = dim // 2
        inv = np.float32(theta) ** (-np.arange(half, dtype=np.float32) / np.float32(half))
        ang = (np.arange(SEQ, dtype=np.float32)[:, None] * inv[None, :]).astype(np.float32)
        co, si = np.cos(ang), np.sin(ang)
        tile = lambda a: a.reshape(TT, P, dim).transpose(1, 0, 2).reshape(P, TT * dim)
        return tile(np.concatenate([co, co], 1)), tile(np.concatenate([-si, si], 1))

    c[:, C_COSR:C_COSR + 128], c[:, C_SINR:C_SINR + 128] = rotary(64, 10000.0)
    c[:, C_COSO:C_COSO + 32], c[:, C_SINO:C_SINO + 32] = rotary(ROT, 500000.0)
    c[:, C_REV:C_REV + 4] = [4, 3, 2, 1]
    c[:, C_PM] = i % BLK
    dec = np.zeros((P, RH, SEQ), np.float64)
    q = np.arange(SEQ)
    for n, h in enumerate((0, 2, 1, 3)):
        g = 1.0 - 2.0 ** (-5.0 - h)
        seen = (q // CHUNK)[None, :] >= (i // CHUNK)[:, None]
        dec[:, n] = np.where(seen, g ** np.abs(q[None, :] - i[:, None]), 0.0) * HD ** -0.5
    return c, dec.reshape(P, RH * SEQ).astype(np.float32)


def bcast(row):
    return bass.AP(row.tensor, row.offset, [[0, P], *[list(d) for d in row.ap[1:]]])


def toeplitz(rel_rows):
    return bass.AP(rel_rows.tensor, 0, [[1, P], [REL_W, CH], [1, 2 * P]])


def head0(g, i):
    return g + 2 * i if g < 2 else (g - 2) // 2 + 2 * (2 * ((g - 2) % 2) + i)


def odd_heads(g):
    if g < 4:
        return 0, [g % 2 + 2 * (4 * (g // 2) + i) for i in range(4)]
    return 1, [(g - 4) % 2 + 2 * (2 * ((g - 4) // 2) + i) for i in range(2)]


OV_STEPS = {"products": ["gate", "up", "turned", "y_left", "y_right", "scattered"],
            "copies": ["rows", "tanh", "high_left", "high_right"],
            "vectors": ["ag", "act", "first_onehots", "onehots", "gated", "low_left", "low_right"]}


def ov_count(b, step):
    name = next(n for n in OV_STEPS if step in OV_STEPS[n])
    return name, b * len(OV_STEPS[name]) + (OV_STEPS[name].index(step) + 1)


def build(nc, x, p, norm_mix, norm_ffn, norm_ple, final_norm, even_w_in, even_ret_gn, even_rel_bias, even_w_out,
          odd_w_qkv, odd_b_qkv, odd_sinks, odd_w_out, odd_b_out, moe_w_group, moe_b_group, moe_w_router,
          moe_b_router, moe_w_gate, moe_w_up, moe_w_down, ple_w_proj, ple_w_gate, const, decay, flip, out, rel_rows):
    wg_d = moe_w_gate.rearrange("l g e d f -> (l g e) d f")
    wu_d = moe_w_up.rearrange("l g e d f -> (l g e) d f")
    wd_d = moe_w_down.rearrange("l g e f d -> (l g e) f d")

    with ExitStack() as ctx:
        def sb(name, shape, dt=F32):
            return ctx.enter_context(nc.sbuf_tensor(name, shape, dt))

        named = {}

        def sem(name):
            if name not in named:
                named[name] = ctx.enter_context(nc.semaphore(name))
            return named[name]

        W = sb("weights", [P, NSLOT, UN])
        H = sb("residual", [P, TT, D])
        XB = sb("normalised", [P, 2 * TT * D])
        AR = sb("arena", [P, 8192])
        C = sb("constants", [P, C_N])
        NW = sb("norm_weights", [P, 6, KD])
        GN = sb("ret_gn", [P, 4])
        WR = sb("router_weights", [P, 2, KD, 20])
        BR = sb("router_bias", [P, 2, 20])
        SK = sb("sinks", [P, SH])
        ST = sb("norm_stats", [P, 8])
        HALF = sb("minus_half", [P, 8])
        RT = sb("router_temps", [P, 480])
        TBL = sb("block_table", [1, 17 + 2 * MAXOV], I32)
        XHL = sb("rows_split", [P, 2, KD, 2 * BLK], F32R)
        Y2 = sb("outputs_split", [P, D], F32R)
        PT2 = sb("scatter_onehots", [P, 2, SEQ], F32R)
        ZEROS = sb("zeros", [1, P], F32R)[:, :]
        with nc.sbuf_tensor("mixer_scratch", [P, 2 * UN], F32) as SCRT:
            pass
        HL = sb("weights_split", [P, NCH, 2, 2, FF], F32R)
        SM = RT[:, 80:144].rearrange("p (n h) -> p n h", n=4)
        ES = RT[:, 144:176].rearrange("p (t h) -> p t h", t=TT)
        B = [ctx.enter_context(nc.psum_tensor(f"bank{n}", [P, 512], F32)) for n in range(8)]

        HS = XB[:, 0:TT * D].rearrange("p (t d) -> p t d", t=TT)
        XT = XB[:, TT * D:2 * TT * D].rearrange("p (k s) -> p k s", k=KD)
        ident = C[:, C_ID:C_ID + P]

        def ar(a, b):
            return AR[:, a:b]

        SCR = SCRT[:, :]
        AQT = ar(0, 1024).rearrange("p (c s) -> p c s", c=4)
        AKT = ar(1024, 2048).rearrange("p (c s) -> p c s", c=4)
        AV = ar(2048, 3072).rearrange("p (t n) -> p t n", t=TT)
        RT4 = ar(3072, 4096).rearrange("p (c s) -> p c s", c=4)
        RVV = ar(4096, 5120).rearrange("p (t n) -> p t n", t=TT)
        GATE = ar(5120, 6144).rearrange("p (t n) -> p t n", t=TT)
        MIXA = ar(6144, 7168).rearrange("p (t n) -> p t n", t=TT)
        RET = ar(7168, 8192).rearrange("p (t n) -> p t n", t=TT)
        RP0 = ar(0, 1024).rearrange("p (h s) -> p h s", h=RH)
        RP1 = ar(1024, 1536).rearrange("p (h s) -> p h s", h=RH)
        STG = [XB[:, n * 1024:(n + 1) * 1024].rearrange("p (t n) -> p t n", t=TT) for n in range(2)]
        REL = AR[0:CH, 7168:7168 + 768]
        TOEP = ar(0, 2048)
        FLIP = ar(2048, 2048 + P)
        BIAS = SCR[:, 0:2048].rearrange("p (h s) -> p h s", h=CH)
        DEC = SCR[:, 2048:3072].rearrange("p (h s) -> p h s", h=RH)
        SC0 = [SCR[:, 3072 + 512 * n:3584 + 512 * n] for n in range(2)]
        PT0 = [SCR[:, 4096 + 512 * n:4608 + 512 * n] for n in range(2)]
        RRO = SCR[:, 5120:6144].rearrange("p (t n) -> p t n", t=TT)
        RTB = SCR[:, 6144:7168].rearrange("p (t n) -> p t n", t=TT)
        THR = SCR[:, 7168:8192].rearrange("p (t n) -> p t n", t=TT)
        BNS = RT[:, 0:48].rearrange("p (t h n) -> p t h n", t=TT, h=RH)
        BNA = RT[:, 48:64].rearrange("p (t h n) -> p t h n", t=TT, h=RH)
        BNE = RT[:, 64:72]
        BNR = RT[:, 72:80]

        Q1 = ar(0, 2048).rearrange("p (t n) -> p t n", t=TT)
        Q1T = ar(2048, 4096).rearrange("p (c s) -> p c s", c=8)
        KV = ar(4096, 4608).rearrange("p (t n) -> p t n", t=TT)
        KDUP = ar(4608, 5120).rearrange("p (t g r n) -> p t g r n", t=TT, g=SKV, r=2)
        K1T = ar(5120, 5632).rearrange("p (g s) -> p g s", g=SKV)
        BQ = ar(5632, 6912)
        BO = ar(5632, 6656)
        RB1 = ar(6912, 7488).rearrange("p (t h n) -> p t h n", t=TT, h=SH + SKV)
        SC1 = [ar(512 * n, 512 * n + 512) for n in range(2)]
        PT1 = [ar(1024 + 512 * n, 1536 + 512 * n) for n in range(2)]
        MIX1 = HS

        XS = XB[:, 0:KD * SLOTS].rearrange("p (k s) -> p k s", k=KD)
        IOTA = ar(0, SLOTS)
        PH = XHL[:, 0, :, :].rearrange("p k s -> p (k s)").rearrange("p (t s) -> p t s", t=TT)
        HSP = [HL[:, 2 + part].rearrange("p a k f -> p (a k f)").rearrange("p (t d) -> p t d", t=TT) for part in range(2)]
        GM = ar(1536, 2560).rearrange("p (t s) -> p t s", t=TT)
        TMP = ar(2560, 3584).rearrange("p (t s) -> p t s", t=TT)
        GRID = [ar(2560 + 128 * n, 2688 + 128 * n) for n in range(6)]
        SROW = ar(3584, 4096).rearrange("p (c s) -> p c s", c=2)
        GR = ar(4096, 4096 + SLOTS)
        ACTT = ar(4672, 4928).rearrange("p (f s) -> p f s", f=KF)
        TG, GSUM, TH, TU, AG, US = (AR[0:BLK, 4928 + 512 * n:5440 + 512 * n] for n in range(6))
        PTMP = ar(0, SEQ)
        XO = ar(2048, 2048 + KD * BLK).rearrange("p (k s) -> p k s", k=KD)
        PIN = ar(0, 512).rearrange("p (t n) -> p t n", t=TT)
        PINT = ar(512, 1024).rearrange("p (k s) -> p k s", k=2)
        THG = ar(1024, 3072).rearrange("p (t n) -> p t n", t=TT)
        FW = ar(3072, 4096)
        OUTB = ar(4096, 6144).rearrange("p (t n) -> p t n", t=TT)

        def unit(n):
            return W[:, n % NSLOT, :]

        def used(n):
            for l, u0 in ((0, U_MOE0), (1, U_MOE1)):
                if u0 <= n < u0 + 3 * NE:
                    e, m = divmod(n - u0, 3)
                    if m == 2:
                        return [("y_ready", 2 * (NE * l + e + 1))]
                    v = 4 * (2 * (NE * l + e) + m + 1)
                    return [("hi_split", v), ("lo_split", v)]
            return [("units_used", n + 1 - 3 * NE * ((n > U_MOE0) + (n > U_MOE1)))]

        def landed(n):
            return sem(f"slot{n % NSLOT}_landed"), 16 * (n // NSLOT + 1)

        def ov_sem(l, name):
            return sem(f"ov{l}_{name}")

        def ov_wait(engine, l, b, step):
            name, value = ov_count(b, step)
            engine.wait_ge(ov_sem(l, name), value)

        block = ctx.enter_context(nc.Block())

        @block.sync
        def _(sp):
            def reusable(n):
                m = n - NSLOT
                if m < 0:
                    return
                for name, value in used(m):
                    sp.wait_ge(sem(name), value)

            def put(n, dst, src):
                reusable(n)
                sp.dma_start(dst, src).then_inc(landed(n)[0], 16)

            def cols(n, w, a, width=512):
                put(n, unit(n)[:, 0:KD * width].rearrange("p (k n) -> p k n", k=KD),
                    w[:, a:a + width].rearrange("(p k) n -> p k n", p=P))

            def rows(n, w, a):
                put(n, unit(n).rearrange("p (k n) -> p k n", k=KD), w[:, a:a + 512].rearrange("(k p) n -> p k n", p=P))

            def load(srcs, e, m, dst, done):
                s = srcs[m][e]
                if m < 2:
                    sp.dma_start(dst, s.rearrange("(p k) f -> p (k f)", p=P)).then_inc(done, 16)
                else:
                    sp.dma_start(dst.rearrange("p (k d) -> p k d", k=KF), s.rearrange("(k p) d -> p k d", p=P))\
                        .then_inc(done, 16)

            def experts(l, u0):
                srcs = (wg_d, wu_d, wd_d)
                for e in range(2):
                    for m in range(3):
                        reusable(u0 + 3 * e + m)
                        load(srcs, l * NE + e, m, unit(u0 + 3 * e + m), landed(u0 + 3 * e + m)[0])
                with sp.Fori(0, NE // 2 - 1) as i:
                    for j in range(2):
                        e = i * 2 + j
                        for m in range(3):
                            n = u0 + 3 * (j + 2) + m
                            if m < 2:
                                sp.wait_ge(sem("hi_split"), e * 8 + (128 * l + 4 * m + 4))
                                sp.wait_ge(sem("lo_split"), e * 8 + (128 * l + 4 * m + 4))
                            else:
                                sp.wait_ge(sem("y_ready"), e * 2 + (32 * l + 2))
                            load(srcs, i * 2 + (l * NE + 2 + j), m, unit(n), landed(n)[0])
                sp.wait_ge(sem("table_ready"), 2 * l + 2)
                novf = sp.value_load(TBL[0:1, 16:17], min_val=0, max_val=MAXOV - 1)
                with sp.If(novf > 0):
                    sp.wait_ge(sem("y_ready"), 32 * (l + 1))
                    sp.wait_ge(sem("hi_split"), 128 * (l + 1))
                    sp.wait_ge(sem("lo_split"), 128 * (l + 1))
                    sp.wait_ge(ov_sem(l, "used"), 1)
                    with sp.Fori(0, novf) as b:
                        e = sp.value_load(TBL[0:1, bass.ds(b + (17 + MAXOV), 1)], min_val=0, max_val=NE - 1)
                        sp.wait_ge(ov_sem(l, "used"), b + 1)
                        for m in range(3):
                            load(srcs, e + l * NE, m, W[:, m, :], ov_sem(l, "landed"))
                    sp.wait_ge(sem("moe_ready"), l + 1)

            sp.dma_start(H[:, :, :], x[0].rearrange("(t p) d -> p t d", p=P)).then_inc(sem("x_landed"), 16)
            sp.dma_start(C[:, :], const).then_inc(sem("const_landed"), 16)
            cols(U_IN, even_w_in[0], 1536)
            sp.wait_ge(sem("bias_landed"), 32)
            order = [1536, 2048, 2560, 0, 512, 1024]
            for u in range(1, 6):
                cols(U_IN + u, even_w_in[0], order[u])
            rows(U_OUT0, even_w_out[0], 0)
            rows(U_OUT0 + 1, even_w_out[0], 512)
            experts(0, U_MOE0)

            def ple(l, n):
                put(n, unit(n)[:, 0:2 * D].rearrange("p (k n) -> p k n", k=2),
                    ple_w_proj[l].rearrange("(k p) n -> p k n", p=P))
                for c in range(2):
                    cols(n + 1 + c, ple_w_gate[l], 512 * c)

            ple(0, U_PLE0)
            cols(U_QKV, odd_w_qkv[0], 0)
            cols(U_QKV + 1, odd_w_qkv[0], 512)
            cols(U_QKV + 2, odd_w_qkv[0], 1024, 256)
            rows(U_OUT1, odd_w_out[0], 0)
            rows(U_OUT1 + 1, odd_w_out[0], 512)
            experts(1, U_MOE1)
            ple(1, U_PLE1)
            sp.wait_ge(sem("out_ready"), 2)
            sp.dma_start(out[0].rearrange("(t p) d -> p t d", p=P), OUTB).then_inc(sem("stored"), 16)
            sp.wait_ge(sem("stored"), 16)

        @block.gpsimd
        def _(pool):
            pool.memset(ZEROS.bitcast(F32), 0.0).then_inc(sem("zeros_set"), 1)
            pool.memset(HALF[:, :], -0.5).then_inc(sem("half_set"), 1)
            def power(k):
                pool.wait_ge(sem("ms_ready"), k + 1)
                pool.tensor_tensor(ST[:, 4:6], ST[:, 2:4], HALF[:, 0:2], ALU.pow).then_inc(sem("rstd_ready"), 1)

            pool.dma_start(NW[:, 0, :], norm_mix[0].rearrange("(p k) -> p k", p=P)).then_inc(sem("first_norm_landed"), 16)
            pool.wait_ge(sem("half_set"), 1)
            power(0)
            small = sem("small_landed")
            for n, w in enumerate((norm_mix, norm_ffn, norm_ple)):
                for l in range(2):
                    if n + l > 0:
                        pool.dma_start(NW[:, 3 * l + n, :], w[l].rearrange("(p k) -> p k", p=P)).then_inc(small, 16)
            pool.dma_start(GN[:, :], even_ret_gn[0].rearrange("(c p) -> p c", p=P),
                           allow_slow_non_contiguous=True).then_inc(small, 16)
            for l in range(2):
                pool.dma_start(WR[:, l, :, 0:4], moe_w_group[l].rearrange("(p k) g -> p k g", p=P)).then_inc(small, 16)
                pool.dma_start(WR[:, l, :, 4:20],
                               moe_w_router[l].rearrange("(p k) g e -> p k (g e)", p=P)).then_inc(small, 16)
                pool.dma_start(BR[:, l, 0:4], bcast(moe_b_group[l:l + 1, :])).then_inc(small, 16)
                pool.dma_start(BR[:, l, 4:20], bcast(moe_b_router[l:l + 1].rearrange("l g e -> l (g e)")))\
                    .then_inc(small, 16)
            pool.dma_start(SK[:, :], bcast(odd_sinks)).then_inc(small, 16)

            def experts(l):
                pool.wait_ge(sem("xT_by_dve"), 2 * (3 * l + 2))
                pool.iota(IOTA, [[1, SLOTS]], base=0, channel_multiplier=0,
                          allow_small_or_imprecise_dtypes=True).then_inc(sem("iota_ready"), 1)
                pool.wait_ge(sem("gr_copied"), l + 1)
                pool.iota(GRID[0], [[1, MAXOV], [0, NE]], base=0, channel_multiplier=0,
                          allow_small_or_imprecise_dtypes=True).then_inc(sem("grids_ready"), 1)
                pool.iota(GRID[1], [[0, MAXOV], [1, NE]], base=0, channel_multiplier=0,
                          allow_small_or_imprecise_dtypes=True).then_inc(sem("grids_ready"), 1)

            pool.wait_ge(sem("gn_ready"), 1)
            pool.tensor_tensor(BNR, BNE, HALF[:, 0:8], ALU.pow).then_inc(sem("gn_rstd"), 1)
            power(1)
            experts(0)
            power(2)
            power(3)
            power(4)
            experts(1)
            power(5)
            power(6)

        @block.tensor
        def _(pe):
            def transposes(k):
                for q in range(4):
                    for kk in range(2):
                        for t in range(TT):
                            if q == 0 and kk == 0:
                                pe.wait_ge(sem("hs_ready"), 2 * k + t + 1)
                            mm = pe.transpose(B[4 + q][:, kk * SEQ + t * P:kk * SEQ + (t + 1) * P],
                                              HS[:, t, 2 * q + kk:D:KD], ident)
                    mm.then_inc(sem("hT_ready"), 1)

            def xt_ready(k):
                pe.wait_ge(sem("xT_by_dve"), 2 * (k + 1))
                pe.wait_ge(sem("xT_by_act"), 2 * (k + 1))

            def project(n, banks, left, width=512, free=None, done=None, t_free=None):
                s, v = landed(n)
                pe.wait_ge(s, v)
                w = unit(n)[:, 0:KD * width].rearrange("p (k n) -> p k n", k=KD)
                for t in range(TT):
                    if free is not None:
                        free(t)
                    for k in range(KD):
                        mm = pe.matmul(B[banks[t]][:, 0:width], left[:, k, t * P:(t + 1) * P], w[:, k, :],
                                       start=(k == 0), stop=(k == KD - 1))
                    mm.then_inc(sem(done), 1)
                pe.drain().then_inc(sem("units_used"), 1)

            pe.wait_ge(sem("const_landed"), 16)
            transposes(0)
            xt_ready(0)

            def in_unit(u):
                def free(t):
                    if u >= 2:
                        pe.wait_ge(sem("in_by_dve" if t == 0 else "in_by_act"), u - 1)
                project(U_IN + u, (2 * (u % 2), 2 * (u % 2) + 1), XT, free=free, done="in_ready")

            def turn(src, banks, name):
                for c in range(4):
                    for t in range(TT):
                        mm = pe.transpose(B[banks[c // 2]][:, (c % 2) * SEQ + t * P:(c % 2) * SEQ + (t + 1) * P],
                                          src[:, t, c * P:(c + 1) * P], ident)
                    if c % 2:
                        mm.then_inc(sem(name), 1)

            def even_group(g):
                return (0, [head0(g, i) for i in range(4)], 128) if g < 2 else (1, [head0(g, i) for i in range(2)], 256)

            def scores0(g):
                t, heads, keys = even_group(g)
                if g >= 2:
                    pe.wait_ge(sem("s0_scaled"), g - 1)
                for i, h in enumerate(heads):
                    r = 64 * (h % 2)
                    mm = pe.matmul(B[4 + g % 2][:, i * keys:(i + 1) * keys], AQT[r:r + 64, h // 2, t * P:(t + 1) * P],
                                   AKT[r:r + 64, h // 2, 0:keys], start=True, stop=True)
                mm.then_inc(sem("s0_ready"), 1)

            def probs0(g):
                pe.wait_ge(sem("s0_exp"), sum(len(even_group(n)[1]) for n in range(g + 1)))
                if g >= 1:
                    pe.wait_ge(sem("pt0_copied"), g)
                for i in range(4):
                    mm = pe.transpose(B[6][:, i * P:(i + 1) * P], SC0[g % 2][:, i * P:(i + 1) * P], ident)
                mm.then_inc(sem("pt0_ready"), 1)

            def values0(g):
                t, heads, keys = even_group(g)
                pe.wait_ge(sem("pt0_copied"), g + 1)
                if g == 2:
                    pe.wait_ge(sem("att0_out"), 1)
                kt = keys // P
                for i, h in enumerate(heads):
                    for n in range(kt):
                        mm = pe.matmul(B[7][:, h * HD:(h + 1) * HD], PT0[g % 2][:, (i * kt + n) * P:(i * kt + n + 1) * P],
                                       AV[:, n, h * HD:(h + 1) * HD], start=(n == 0), stop=(n == kt - 1))
                mm.then_inc(sem("pv0_ready"), 1)

            in_unit(0)
            pe.wait_ge(sem("bias_landed"), 32)
            for n in range(4):
                pe.matmul(B[4 + n][:, :], FLIP, TOEP[:, n * 512:(n + 1) * 512], start=True, stop=True)\
                    .then_inc(sem("bias_ready"), 1)
            in_unit(1)
            pe.wait_ge(sem("bias_copied"), 4)
            pe.wait_ge(sem("in_by_dve"), 1)
            pe.wait_ge(sem("in_by_act"), 1)
            turn(STG[0], (4, 5), "aqk_turned")
            pe.wait_ge(sem("in_by_dve"), 2)
            pe.wait_ge(sem("in_by_act"), 2)
            turn(STG[1], (6, 7), "aqk_turned")
            in_unit(2)
            pe.wait_ge(sem("aqkT_by_dve"), 2)
            pe.wait_ge(sem("aqkT_by_act"), 2)
            scores0(0)
            scores0(1)
            in_unit(3)
            pe.wait_ge(sem("in_by_dve"), 3)
            pe.wait_ge(sem("in_by_act"), 3)
            probs0(0)
            scores0(2)
            probs0(1)
            values0(0)
            scores0(3)
            in_unit(4)
            values0(1)
            probs0(2)
            scores0(4)
            probs0(3)
            values0(2)
            scores0(5)
            in_unit(5)
            values0(3)
            probs0(4)
            probs0(5)
            values0(4)
            values0(5)
            pe.wait_ge(sem("ret_rotated"), 2)
            turn(RRO, (4, 5), "rqk_turned")
            pe.wait_ge(sem("rqkT_by_dve"), 1)
            pe.wait_ge(sem("rqkT_by_act"), 1)
            pe.wait_ge(sem("pt0_copied"), 6)
            pe.wait_ge(sem("att0_out"), 2)
            for par in range(2):
                r = 64 * par
                for i in range(2):
                    mm = pe.matmul(B[4 + par][:, i * SEQ:(i + 1) * SEQ], RT4[r:r + 64, 2 + i, 0:P], RT4[r:r + 64, i, :],
                                   start=True, stop=True)
                mm.then_inc(sem("rs_ready"), 1)
            for par in range(2):
                r = 64 * par
                for i in range(2):
                    mm = pe.matmul(B[6 + par][:, i * P:(i + 1) * P], RT4[r:r + 64, 2 + i, P:SEQ], RT4[r:r + 64, i, P:SEQ],
                                   start=True, stop=True)
                mm.then_inc(sem("rs_ready"), 1)
            pe.wait_ge(sem("rs_decayed"), 4)
            pe.wait_ge(sem("in_by_dve"), 5)
            pe.wait_ge(sem("in_by_act"), 5)
            for t in range(TT):
                for n in range(RH):
                    h = (0, 2, 1, 3)[n]
                    dst, v = B[t][:, h * RV:(h + 1) * RV], slice(h * RV, (h + 1) * RV)
                    mm = pe.matmul(dst, RP0[:, n, t * P:(t + 1) * P], RVV[:, 0, v], start=True, stop=(t == 0))
                    if t:
                        mm = pe.matmul(dst, RP1[:, n, :], RVV[:, 1, v], start=False, stop=True)
                mm.then_inc(sem("ro_ready"), 1)
            turn(MIXA, (6, 7), "mix0_turned")
            pe.wait_ge(sem("ret_out"), 2)
            turn(RET, (4, 5), "mix0_turned")
            pe.wait_ge(sem("mix0T_by_dve"), 2)
            pe.wait_ge(sem("mix0T_by_act"), 2)
            project(U_OUT0, (0, 1), XT, done="out0_ready")
            project(U_OUT0 + 1, (2, 3), XT, done="out0_ready")

            def experts(l, u0):
                kn = 3 * l + 1
                transposes(kn)
                xt_ready(kn)
                if l == 0:
                    pe.wait_ge(sem("small_landed"), 15 * 16)
                for t in range(TT):
                    for k in range(KD):
                        mm = pe.matmul(B[0][:, t * 20:(t + 1) * 20], XT[:, k, t * P:(t + 1) * P], WR[:, l, k, :],
                                       start=(k == 0), stop=(k == KD - 1))
                mm.then_inc(sem("logits_ready"), 1)
                pe.wait_ge(sem("chosen"), l + 1)
                M = RT[:, 100:132].rearrange("p (t e) -> p t e", t=TT)
                low, one = C[:, C_LOW:C_LOW + P], C[:, C_ONE:C_ONE + P]
                pe.matmul(B[1][:, 0:NE], low, M[:, 0, :], start=True, stop=True)
                pe.matmul(B[1][:, NE:2 * NE], one, M[:, 0, :], start=True, stop=False)
                pe.matmul(B[1][:, NE:2 * NE], low, M[:, 1, :], start=False, stop=True)
                pe.matmul(B[1][:, 2 * NE:3 * NE], one, M[:, 0, :], start=True, stop=False)
                pe.matmul(B[1][:, 2 * NE:3 * NE], one, M[:, 1, :], start=False, stop=True).then_inc(sem("ranks_ready"), 1)

                pe.wait_ge(sem("slots_ready"), l + 1)
                for c in range(4):
                    mm = pe.matmul(B[2][:, c * P:(c + 1) * P], RT[:, 404 + c:405 + c].to_broadcast([P, P]), ident,
                                   start=True, stop=True)
                mm.then_inc(sem("srow_ready"), 1)
                pe.wait_ge(sem("onehots_ready"), l + 1)
                pe.wait_ge(sem("srow_copied"), l + 1)
                pe.wait_ge(sem("hs_low"), l + 1)
                for k in (4, 5, 6, 7, 0, 1, 2, 3):
                    for part in range(2):
                        for t in range(TT):
                            mm = pe.matmul(B[k][:, :], HSP[part][:, t, k:D:KD], PH[:, t, :], start=(t + part == 0),
                                           stop=(t + part == TT))
                    mm.then_inc(sem("rows_ready"), 1)
                pe.wait_ge(sem("gates_ready"), l + 1)
                pe.wait_ge(sem("rows_by_act"), 4 * l + 3)
                for t in range(TT):
                    mm = pe.matmul(B[0][:, :], one, GM[:, t, :], start=(t == 0), stop=(t == TT - 1))
                mm.then_inc(sem("gr_ready"), 1)
                pe.wait_ge(sem("rows_by_dve"), 4 * (l + 1))
                pe.wait_ge(sem("rows_by_act"), 4 * (l + 1))

                def turned_back(done):
                    for f in range(KF):
                        mm = pe.transpose(B[6][:, f * BLK:(f + 1) * BLK], US[:, f * P:(f + 1) * P], C[0:BLK, C_ID:C_ID + BLK])
                    mm.then_inc(done, 1)

                def down(wd, done):
                    for half in range(2):
                        for f in range(KF):
                            mm = pe.matmul(B[6 + half][0:BLK, :], ACTT[:, f, :], wd[:, f, half * 512:(half + 1) * 512],
                                           start=(f == 0), stop=(f == KF - 1))
                        mm.then_inc(done, 1)

                def scatter(par, start, done):
                    for t in range(TT):
                        for half in range(2):
                            mm = pe.matmul(B[2 * t + half][:, :], PT2[:, par, t * P:(t + 1) * P],
                                           Y2[:, half * 512:(half + 1) * 512], start=start, stop=False)
                    mm.then_inc(done, 1)

                def step(e, lap):
                    def v(per, const):
                        c = per * (NE * l + e) + const
                        return c if lap is None else lap * (2 * per) + c
                    later = l + e > 1 or lap is not None

                    def product(m):
                        for c in range(NCH):
                            pe.wait_ge(sem("hi_split"), v(8, 4 * m + c + 1))
                            pe.wait_ge(sem("lo_split"), v(8, 4 * m + c + 1))
                            for part in range(2):
                                for kk in range(2):
                                    mm = pe.matmul(B[4 + m][:, :], XHL[:, e % 2, 2 * c + kk, :], HL[:, c, part, kk, :],
                                                   start=(c + part + kk == 0), stop=(c == NCH - 1 and part + kk == 2))
                            mm.then_inc(sem("chunk_used"), 1)

                    if e < NE:
                        pe.wait_ge(sem("xl_ready"), v(1, 1))
                        if l + e or lap is not None:
                            pe.wait_ge(sem("gate_folded"), v(1, 0))
                        product(0)
                    if 1 <= e <= NE:
                        pe.wait_ge(sem("act_ready"), v(1, 0))
                        if later:
                            pe.wait_ge(sem("yl_ready"), v(2, -2))
                    if e >= 2:
                        pe.wait_ge(sem("pt2_ready"), v(1, -1))
                        pe.wait_ge(sem("yl_ready"), v(2, -2))
                        if e == 2 and lap is None:
                            pe.wait_ge(sem("gr_copied"), l + 1)
                        scatter(e % 2, e == 2 and lap is None, sem("sc_done"))
                    if 1 <= e <= NE:
                        turned_back(sem("act_turned"))
                    if e < NE:
                        if l + e or lap is not None:
                            pe.wait_ge(sem("up_folded"), v(1, 0))
                        product(1)
                    if 1 <= e <= NE:
                        s, w = landed(u0 + 3 * (e - 1) + 2)
                        pe.wait_ge(s, w if lap is None else lap * 16 + w)
                        pe.wait_ge(sem("actt_ready"), v(1, 0))
                        down(unit(u0 + 3 * (e - 1) + 2).rearrange("p (k d) -> p k d", k=KF), sem("y_ready"))

                for e in range(4):
                    step(e, None)
                with pe.Fori(0, 6) as i:
                    step(4, i)
                    step(5, i)
                for e in (16, 17):
                    step(e, None)

                pe.wait_ge(sem("table_ready"), 2 * l + 2)
                novf = pe.value_load(TBL[0:1, 16:17], min_val=0, max_val=MAXOV - 1)
                with pe.If(novf > 0):
                    pe.drain().then_inc(ov_sem(l, "used"), 1)
                    with pe.Fori(0, novf) as b:
                        pe.wait_ge(ov_sem(l, "landed"), b * 48 + 48)
                        ov_wait(pe, l, b, "rows")
                        for m in range(2):
                            w = W[:, m, :].rearrange("p (k f) -> p k f", k=KD)
                            for k in range(KD):
                                mm = pe.matmul(B[4 + m][0:BLK, :], XO[:, k, :], w[:, k, :], start=(k == 0), stop=(k == KD - 1))
                            mm.then_inc(ov_sem(l, "products"), 1)
                        ov_wait(pe, l, b, "act")
                        pe.matmul(B[7][:, :], PT2[:, 1, 0:P], Y2[:, 0:512], start=True, stop=True)
                        turned_back(ov_sem(l, "products"))
                        ov_wait(pe, l, b, "gated")
                        down(W[:, 2, :].rearrange("p (k d) -> p k d", k=KF), ov_sem(l, "products"))
                        ov_wait(pe, l, b, "low_right")
                        scatter(0, False, ov_sem(l, "products"))
                        pe.drain().then_inc(ov_sem(l, "used"), 1)
                pe.wait_ge(sem("zeros_set"), 1)
                for n in range(4):
                    mm = pe.matmul(B[n][:, :], ZEROS[0:1, :], Y2[0:1, 0:512], start=False, stop=True)
                mm.then_inc(sem("moe_ready"), 1)

            def ple(l, n):
                pe.wait_ge(sem("p_landed"), 16 * (l + 1))
                for k in range(2):
                    for t in range(TT):
                        mm = pe.transpose(B[4][:, k * SEQ + t * P:k * SEQ + (t + 1) * P], PIN[:, t, k * P:(k + 1) * P], ident)
                mm.then_inc(sem("pT_ready"), 1)
                pe.wait_ge(sem("pT_copied"), l + 1)
                s, v = landed(n)
                pe.wait_ge(s, v)
                wp = unit(n)[:, 0:2 * D].rearrange("p (k n) -> p k n", k=2)
                for t in range(TT):
                    for half in range(2):
                        pe.wait_ge(sem("h_updates"), 12 * l + 4 + 2 * t + half + 1)
                        for k in range(2):
                            mm = pe.matmul(B[2 * t + half][:, :], PINT[:, k, t * P:(t + 1) * P],
                                           wp[:, k, half * 512:(half + 1) * 512], start=(k == 0), stop=(k == 1))
                mm.then_inc(sem("pp_ready"), 1)
                pe.drain().then_inc(sem("units_used"), 1)
                transposes(3 * l + 2)
                xt_ready(3 * l + 2)
                project(n + 1, (4, 6), XT, done="pg_ready")
                project(n + 2, (5, 7), XT, done="pg_ready")

            experts(0, U_MOE0)
            ple(0, U_PLE0)

            transposes(3)
            xt_ready(3)

            def res_free(t):
                pe.wait_ge(sem("h_updates"), 12)
            project(U_QKV, (0, 1), XT, free=res_free, done="qkv_ready")
            project(U_QKV + 1, (2, 3), XT, done="qkv_ready")
            project(U_QKV + 2, (4, 5), XT, width=256, done="qkv_ready")
            for t in range(TT):
                pe.wait_ge(sem("q1_rotated"), t + 1)
                for c in range(8):
                    bank = (6, 7, 0, 1)[c // 2]
                    mm = pe.transpose(B[bank][:, (c % 2) * SEQ + t * P:(c % 2) * SEQ + (t + 1) * P],
                                      Q1[:, t, c * P:(c + 1) * P], ident)
                    if t == 1 and c % 2:
                        mm.then_inc(sem("q1_turned"), 1)
                for g in range(SKV):
                    mm = pe.transpose(B[2][:, g * SEQ + t * P:g * SEQ + (t + 1) * P],
                                      KDUP[:, t, g].rearrange("p r n -> p (r n)"), ident)
            mm.then_inc(sem("k1_turned"), 1)
            pe.wait_ge(sem("q1T_by_dve"), 2)
            pe.wait_ge(sem("q1T_by_act"), 2)
            pe.wait_ge(sem("k1T_copied"), 1)

            def odd_group(g):
                t, heads = odd_heads(g)
                return t, heads, (128, 192)[t]

            def scores1(g):
                t, heads, keys = odd_group(g)
                if g >= 2:
                    pe.wait_ge(sem("s1_scaled"), g - 1)
                for i, h in enumerate(heads):
                    r = 64 * (h % 2)
                    mm = pe.matmul(B[4 + g % 2][:, i * keys:(i + 1) * keys], Q1T[r:r + 64, h // 2, t * P:(t + 1) * P],
                                   K1T[r:r + 64, h // 8, 64 * t:64 * t + keys], start=True, stop=True)
                mm.then_inc(sem("s1_ready"), 1)

            def probs1(g):
                pe.wait_ge(sem("s1_exp"), sum(len(odd_group(n)[1]) for n in range(g + 1)))
                if g >= 2:
                    pe.wait_ge(sem("pt1_copied"), g - 1)
                for i in range(4):
                    mm = pe.transpose(B[6 + g % 2][:, i * P:(i + 1) * P], SC1[g % 2][:, i * P:(i + 1) * P], ident)
                mm.then_inc(sem("pt1_ready"), 1)

            def values1(g):
                t, heads, keys = odd_group(g)
                pe.wait_ge(sem("pt1_copied"), g + 1)
                kt = 1 + t
                for i, h in enumerate(heads):
                    for n in range(kt):
                        mm = pe.matmul(B[2 * t + h // 8][:, (h % 8) * HD:(h % 8 + 1) * HD],
                                       PT1[g % 2][:, (i * kt + n) * P:(i * kt + n + 1) * P],
                                       KV[:, n, 128 + (h // 8) * HD:128 + (h // 8 + 1) * HD],
                                       start=(n == 0), stop=(n == kt - 1))
                mm.then_inc(sem("pv1_ready"), 1)

            for g in range(12 + 2):
                if g < 12:
                    scores1(g)
                if 1 <= g <= 12:
                    probs1(g - 1)
                if g >= 2:
                    values1(g - 2)
            for t in range(TT):
                pe.wait_ge(sem("att1_out"), t + 1)
                for c in range(8):
                    mm = pe.transpose(B[4 + c // 2][:, (c % 2) * SEQ + t * P:(c % 2) * SEQ + (t + 1) * P],
                                      MIX1[:, t, c * P:(c + 1) * P], ident)
                    if t == 1 and c % 2:
                        mm.then_inc(sem("mix1_turned"), 1)
            pe.wait_ge(sem("mix1T_by_dve"), 2)
            pe.wait_ge(sem("mix1T_by_act"), 2)
            project(U_OUT1, (0, 1), XT, done="out1_ready")
            project(U_OUT1 + 1, (2, 3), XT, done="out1_ready")
            experts(1, U_MOE1)
            ple(1, U_PLE1)

        @block.scalar
        def _(act):
            def squares(k, src_ready):
                src_ready()
                for t in range(TT):
                    act.activation(HS[:, t, :], H[:, t, :], ACT.Square, accum_out=ST[:, t:t + 1])\
                        .then_inc(sem("squares_ready"), 1)

            def xt_evac(k):
                for q in (1, 3):
                    act.wait_ge(sem("hT_ready"), 4 * k + q + 1)
                    for kk in range(2):
                        i = act.activation(XT[:, 2 * q + kk, :], B[4 + q][:, kk * SEQ:(kk + 1) * SEQ], ACT.Copy,
                                           scale=NW[:, k, 2 * q + kk:2 * q + kk + 1])
                    i.then_inc(sem("xT_by_act"), 1)

            def copy(dst, src):
                return act.activation(dst, src, ACT.Copy)

            act.dma_start(REL[:, 0:257], even_rel_bias[0]).then_inc(sem("rel_landed"), 16)
            squares(0, lambda: act.wait_ge(sem("x_landed"), 16))
            act.wait_ge(sem("rel_reversed"), 2)
            act.dma_start(rel_rows, REL[:, 384:384 + REL_W]).then_inc(sem("rel_stored"), 16)
            act.wait_ge(sem("rel_stored"), 16)
            act.dma_start(FLIP, flip).then_inc(sem("bias_landed"), 16)
            act.dma_start(TOEP.rearrange("p (h s) -> p h s", h=CH), toeplitz(rel_rows)).then_inc(sem("bias_landed"), 16)

            act.dma_start(DEC.rearrange("p h s -> p (h s)"), decay).then_inc(sem("decay_landed"), 16)

            act.wait_ge(sem("first_norm_landed"), 16)
            xt_evac(0)

            dst = {0: STG[0], 1: STG[1], 2: AV, 3: STG[0], 4: RVV}

            def in_evac(u):
                act.wait_ge(sem("in_ready"), 2 * u + 2)
                if u == 3:
                    act.wait_ge(sem("aqk_turned"), 2)
                copy(dst[u][:, 1, :], B[2 * (u % 2) + 1][:, :]).then_inc(sem("in_by_act"), 1)

            def even_heads(g):
                return (4, 128) if g < 2 else (2, 256)

            def exps0(g):
                nh, keys = even_heads(g)
                act.wait_ge(sem("max0_ready"), g + 1)
                for i in range(nh):
                    h = head0(g, i)
                    t = 0 if g < 2 else 1
                    s = SC0[g % 2][:, i * keys:(i + 1) * keys]
                    act.activation(s, s, ACT.Exp, bias=SM[:, t, h:h + 1], accum_out=SM[:, 2 + t, h:h + 1])\
                        .then_inc(sem("s0_exp"), 1)

            def pt_evac0(g):
                act.wait_ge(sem("pt0_ready"), g + 1)
                if g >= 2:
                    act.wait_ge(sem("pv0_ready"), g - 1)
                copy(PT0[g % 2][:, :], B[6][:, :]).then_inc(sem("pt0_copied"), 1)

            in_evac(0)
            in_evac(1)
            act.wait_ge(sem("aqk_turned"), 2)
            copy(AQT[:, 2:4, :].rearrange("p c s -> p (c s)"), B[5][:, :]).then_inc(sem("aqkT_by_act"), 1)
            act.wait_ge(sem("aqk_turned"), 4)
            copy(AKT[:, 2:4, :].rearrange("p c s -> p (c s)"), B[7][:, :]).then_inc(sem("aqkT_by_act"), 1)
            in_evac(2)
            exps0(0)
            exps0(1)
            in_evac(3)
            pt_evac0(0)
            pt_evac0(1)
            exps0(2)
            exps0(3)
            in_evac(4)
            pt_evac0(2)
            pt_evac0(3)
            exps0(4)
            exps0(5)
            for t in range(TT):
                act.wait_ge(sem("in_ready"), 10 + t + 1)
                act.activation(THR[:, t, :], B[2 + t][:, :], ACT.Tanh, scale=0.5).then_inc(sem("rg_tanh"), 1)
            pt_evac0(4)
            pt_evac0(5)
            act.wait_ge(sem("rqk_turned"), 2)
            copy(RT4[:, 2:4, :].rearrange("p c s -> p (c s)"), B[5][:, :]).then_inc(sem("rqkT_by_act"), 1)
            act.wait_ge(sem("mix0_turned"), 2)
            copy(XT[:, 6:8, :].rearrange("p c s -> p (c s)"), B[7][:, :]).then_inc(sem("mix0T_by_act"), 1)
            act.wait_ge(sem("mix0_turned"), 4)
            act.wait_ge(sem("gn_halved"), 1)
            for c in range(2):
                i = act.activation(XT[:, 2 + c, :], B[5][:, c * SEQ:(c + 1) * SEQ], ACT.Copy, scale=GN[:, 2 + c:3 + c])
            i.then_inc(sem("mix0T_by_act"), 1)

            def h_ready(n):
                return lambda: act.wait_ge(sem("h_updates"), 4 * n)

            def experts(l, u0):
                kn = 3 * l + 1
                squares(kn, h_ready(3 * l + 1))
                xt_evac(kn)
                for t in range(TT):
                    copy(HSP[0][:, t, :], HS[:, t, :]).then_inc(sem("hs_high"), 1)
                act.wait_ge(sem("g_below_max"), l + 1)
                act.activation(RT[:, 20:28], RT[:, 20:28], ACT.Exp).then_inc(sem("g_exp"), 1)
                act.wait_ge(sem("second_below_first"), l + 1)
                act.activation(RT[:, 84:86], RT[:, 84:86], ACT.Exp).then_inc(sem("second_exp"), 1)
                act.wait_ge(sem("srow_ready"), l + 1)
                copy(SROW.rearrange("p c s -> p (c s)"), B[2][:, :]).then_inc(sem("srow_copied"), 1)

                def high(n, lap, e, m, chunks=range(NCH)):
                    at = lambda c: c if lap is None else lap * 16 + c
                    s, w = landed(n)
                    act.wait_ge(s, at(w))
                    for c in chunks:
                        j = 8 * (NE * l + e) + 4 * m + c
                        if j >= NCH:
                            act.wait_ge(sem("chunk_used"), at(j - NCH + 1))
                        copy(HL[:, c, 0, :, :].rearrange("p k f -> p (k f)"), unit(n)[:, c * 1024:(c + 1) * 1024])\
                            .then_inc(sem("hi_split"), 1)

                def rows(e, lap):
                    at = lambda per, const: (per * (NE * l + e) + const) if lap is None \
                        else lap * (2 * per) + (per * (NE * l + e) + const)
                    off = act.value_load(TBL[0:1, bass.ds(at(1, -NE * l), 1)], min_val=0, max_val=LAST)
                    if NE * l + e >= 2:
                        act.wait_ge(sem("chunk_used"), at(8, -8))
                    act.activation(XHL[:, e % 2, :, 0:BLK], XS[:, :, bass.ds(off, BLK)], ACT.Copy)\
                        .then_inc(sem("xh_ready"), 1)

                high(u0, None, 0, 0, (0, 1))
                for k in (4, 5, 0, 1):
                    act.wait_ge(sem("rows_ready"), 8 * l + (k - 3 if k > 3 else 8))
                    act.activation(XS[:, k, :], B[k][:, :], ACT.Copy, scale=NW[:, kn, k:k + 1]).then_inc(sem("rows_by_act"), 1)
                act.wait_ge(sem("rows_by_act"), 4 * (l + 1))
                act.wait_ge(sem("rows_by_dve"), 4 * (l + 1))
                act.wait_ge(sem("table_ready"), 2 * l + 1)
                rows(0, None)
                high(u0, None, 0, 0, (2, 3))
                act.wait_ge(sem("gr_ready"), l + 1)
                act.activation(GR, B[0][:, :], ACT.Copy, scale=0.5).then_inc(sem("gr_copied"), 1)

                def outputs(banks_ready, done, value):
                    for half in range(2):
                        c = slice(half * 512, (half + 1) * 512)
                        act.wait_ge(banks_ready, value(half))
                        copy(Y2[0:BLK, c], B[6 + half][0:BLK, :]).then_inc(done, 1)

                def step(e, lap):
                    def v(per, const):
                        c = per * (NE * l + e) + const
                        return c if lap is None else lap * (2 * per) + c
                    if e < NE:
                        high(u0 + 3 * e + 1, lap, e, 1)
                        act.wait_ge(sem("chunk_used"), v(8, 4))
                        copy(TG, B[4][BLK:P, :]).then_inc(sem("gate_low"), 1)
                        act.wait_ge(sem("gate_folded"), v(1, 1))
                        act.activation(TH, GSUM, ACT.Tanh, scale=0.5).then_inc(sem("th_ready"), 1)
                        act.wait_ge(sem("chunk_used"), v(8, 8))
                        copy(TU, B[5][BLK:P, :]).then_inc(sem("up_low"), 1)
                    if e < NE - 1:
                        rows(e + 1, lap)
                        high(u0 + 3 * e + 3, lap, e + 1, 0)
                    if 1 <= e <= NE:
                        if l + e > 1 or lap is not None:
                            act.wait_ge(sem("sc_done"), v(1, -1))
                        outputs(sem("y_ready"), sem("yh_ready"), lambda half: v(2, half - 1))

                for e in range(4):
                    step(e, None)
                with act.Fori(0, 5) as i:
                    step(4, i)
                    step(5, i)
                for e in (14, 15, 16):
                    step(e, None)

                act.wait_ge(sem("table_ready"), 2 * l + 2)
                novf = act.value_load(TBL[0:1, 16:17], min_val=0, max_val=MAXOV - 1)
                with act.If(novf > 0):
                    act.wait_ge(sem("sc_done"), NE * (l + 1))
                    with act.Fori(0, novf) as b:
                        off = act.value_load(TBL[0:1, bass.ds(b + 17, 1)], min_val=0, max_val=LAST)
                        act.wait_ge(ov_sem(l, "used"), b + 1)
                        copy(XO, XS[:, :, bass.ds(off, BLK)]).then_inc(ov_sem(l, "copies"), 1)
                        ov_wait(act, l, b, "gate")
                        act.activation(TH, B[4][0:BLK, :], ACT.Tanh, scale=0.5).then_inc(ov_sem(l, "copies"), 1)
                        outputs(ov_sem(l, "products"), ov_sem(l, "copies"), lambda half: ov_count(b, ("y_left", "y_right")[half])[1])

            def ple(l):
                act.wait_ge(sem("h_updates"), 12 * l + 8)
                act.dma_start(PIN, p[l, 0].rearrange("(t p) d -> p t d", p=P)).then_inc(sem("p_landed"), 16)
                if l == 1:
                    act.dma_start(FW, bcast(final_norm.rearrange("(a d) -> a d", a=1))).then_inc(sem("fw_landed"), 16)
                squares(3 * l + 2, h_ready(3 * l + 2))
                act.wait_ge(sem("pT_ready"), l + 1)
                copy(PINT.rearrange("p k s -> p (k s)"), B[4][:, :]).then_inc(sem("pT_copied"), 1)
                xt_evac(3 * l + 2)
                for half in range(2):
                    for t in range(TT):
                        act.wait_ge(sem("pg_ready"), 4 * l + 2 * half + t + 1)
                        act.activation(THG[:, t, half * 512:(half + 1) * 512], B[4 + half + 2 * t][:, :], ACT.Tanh,
                                       scale=0.5).then_inc(sem("pg_tanh"), 1)

            experts(0, U_MOE0)
            ple(0)

            act.wait_ge(sem("h_updates"), 12)
            act.dma_start(BQ, bcast(odd_b_qkv)).then_inc(sem("bq_landed"), 16)
            squares(3, h_ready(3))
            xt_evac(3)
            act.wait_ge(sem("q1_turned"), 2)
            copy(Q1T[:, 2:4, :].rearrange("p c s -> p (c s)"), B[7][:, :]).then_inc(sem("q1T_by_act"), 1)
            act.wait_ge(sem("q1_turned"), 4)
            copy(Q1T[:, 6:8, :].rearrange("p c s -> p (c s)"), B[1][:, :]).then_inc(sem("q1T_by_act"), 1)
            act.dma_start(BO, bcast(odd_b_out)).then_inc(sem("bo_landed"), 16)

            def exps1(g):
                act.wait_ge(sem("max1_ready"), g + 1)
                t, heads = odd_heads(g)
                for i, h in enumerate(heads):
                    s = SC1[g % 2][:, i * 128:(i + 1) * 128] if t == 0 else SC1[g % 2][:, i * 256 + 64:(i + 1) * 256]
                    act.activation(s, s, ACT.Exp, bias=SM[:, t, h:h + 1], accum_out=SM[:, 2 + t, h:h + 1])\
                        .then_inc(sem("s1_exp"), 1)

            def pt_evac1(g):
                act.wait_ge(sem("pt1_ready"), g + 1)
                if g >= 2:
                    act.wait_ge(sem("pv1_ready"), g - 1)
                copy(PT1[g % 2][:, :], B[6 + g % 2][:, :]).then_inc(sem("pt1_copied"), 1)

            for g in range(13):
                if g < 12:
                    exps1(g)
                if g >= 1:
                    pt_evac1(g - 1)
            for t in range(TT):
                act.wait_ge(sem("sink_below_max"), t + 1)
                act.activation(ES[:, t, :], ES[:, t, :], ACT.Exp).then_inc(sem("sink_exp"), 1)
            for q in (1, 3):
                act.wait_ge(sem("mix1_turned"), q + 1)
                copy(XT[:, 2 * q:2 * q + 2, :].rearrange("p c s -> p (c s)"), B[4 + q][:, :])\
                    .then_inc(sem("mix1T_by_act"), 1)
            experts(1, U_MOE1)
            ple(1)
            squares(6, h_ready(6))

        @block.vector
        def _(dve):
            steps = [0]

            def then(ins):
                steps[0] += 1
                ins.then_inc(sem("dve_steps"), 1)
                dve.wait_ge(sem("dve_steps"), steps[0])

            def norm(k):
                dve.wait_ge(sem("squares_ready"), 2 * (k + 1))
                dve.tensor_scalar(ST[:, 2:4], ST[:, 0:2], 1.0 / D, EPS, ALU.mult, ALU.add).then_inc(sem("ms_ready"), 1)
                dve.wait_ge(sem("rstd_ready"), k + 1)
                for t in range(TT):
                    if k < 6:
                        dve.tensor_scalar(HS[:, t, :], H[:, t, :], ST[:, 4 + t:5 + t], None, ALU.mult)\
                            .then_inc(sem("hs_ready"), 1)

            def xt_evac(k):
                for q in (0, 2):
                    dve.wait_ge(sem("hT_ready"), 4 * k + q + 1)
                    dve.tensor_tensor(XT[:, 2 * q:2 * q + 2, :], B[4 + q][:, :].rearrange("p (k s) -> p k s", k=2),
                                      NW[:, k, 2 * q:2 * q + 2].unsqueeze(2).to_broadcast([P, 2, SEQ]), ALU.mult)\
                        .then_inc(sem("xT_by_dve"), 1)

            dve.wait_ge(sem("rel_landed"), 16)
            dve.tensor_copy(REL[:, 384 + 127:384 + REL_W], REL[:, 256:0:-1]).then_inc(sem("rel_reversed"), 1)
            dve.tensor_copy(REL[:, 384:384 + 127], REL[:, 256:257].to_broadcast([CH, 127])).then_inc(sem("rel_reversed"), 1)
            norm(0)
            dve.wait_ge(sem("first_norm_landed"), 16)
            xt_evac(0)

            dst = {0: STG[0], 1: STG[1], 2: AV, 3: STG[0], 4: RVV}

            def in_evac(u):
                dve.wait_ge(sem("in_ready"), 2 * u + 1)
                if u == 3:
                    dve.wait_ge(sem("aqk_turned"), 2)
                dve.tensor_copy(dst[u][:, 0, :], B[2 * (u % 2)][:, :]).then_inc(sem("in_by_dve"), 1)

            def scale0(g):
                t = 0 if g < 2 else 1
                nh, keys = (4, 128) if t == 0 else (2, 256)
                h0 = head0(g, 0)
                dve.wait_ge(sem("s0_ready"), g + 1)
                if g >= 2:
                    dve.wait_ge(sem("pt0_ready"), g - 1)
                sc = SC0[g % 2].rearrange("p (h s) -> p h s", h=nh)
                dve.scalar_tensor_tensor(out=sc, in0=B[4 + g % 2][:, :].rearrange("p (h s) -> p h s", h=nh),
                                         scalar=HD ** -0.5, in1=BIAS[:, h0:h0 + 2 * nh - 1:2, 256 - keys:256],
                                         op0=ALU.mult, op1=ALU.add).then_inc(sem("s0_scaled"), 1)
                dve.wait_ge(sem("s0_scaled"), g + 1)
                dve.tensor_reduce(SM[:, t, h0:h0 + 2 * nh - 1:2], sc, AX.X, ALU.max, negate=True)\
                    .then_inc(sem("max0_ready"), 1)

            def att_out0(t):
                dve.wait_ge(sem("s0_exp"), 8 * (t + 1))
                then(dve.reciprocal(SM[:, 2 + t, 0:CH], SM[:, 2 + t, 0:CH]))
                dve.wait_ge(sem("pv0_ready"), 2 + 4 * t)
                dve.tensor_tensor(MIXA[:, t, :].rearrange("p (h n) -> p h n", h=CH),
                                  B[7][:, :].rearrange("p (h n) -> p h n", h=CH),
                                  SM[:, 2 + t, 0:CH].unsqueeze(2).to_broadcast([P, CH, HD]), ALU.mult)\
                    .then_inc(sem("att0_out"), 1)

            in_evac(0)
            for n in range(4):
                dve.wait_ge(sem("bias_ready"), n + 1)
                src = B[4 + n][:, :].rearrange("p (h s) -> p h s", h=2)
                dve.tensor_copy(BIAS[:, 2 * n:2 * n + 2, 0:128], src[:, :, 0:128])
                dve.tensor_tensor(BIAS[:, 2 * n:2 * n + 2, 128:256], src[:, :, 128:256],
                                  C[:, C_M0:C_M0 + P].unsqueeze(1).to_broadcast([P, 2, P]), ALU.add)\
                    .then_inc(sem("bias_copied"), 1)
            in_evac(1)
            dve.wait_ge(sem("aqk_turned"), 1)
            dve.tensor_copy(AQT[:, 0:2, :].rearrange("p c s -> p (c s)"), B[4][:, :]).then_inc(sem("aqkT_by_dve"), 1)
            dve.wait_ge(sem("aqk_turned"), 3)
            dve.tensor_copy(AKT[:, 0:2, :].rearrange("p c s -> p (c s)"), B[6][:, :]).then_inc(sem("aqkT_by_dve"), 1)
            in_evac(2)
            dve.wait_ge(sem("bias_copied"), 4)
            scale0(0)
            scale0(1)
            dve.wait_ge(sem("small_landed"), 15 * 16)
            dve.tensor_scalar(GN[:, :], GN[:, :], 0.5, None, ALU.mult).then_inc(sem("gn_halved"), 1)
            in_evac(3)
            scale0(2)
            scale0(3)
            att_out0(0)

            def rotate(t):
                cosr = C[:, C_COSR + 64 * t:C_COSR + 64 * t + 64].unsqueeze(1).to_broadcast([P, 8, 64])
                sinr = C[:, C_SINR + 64 * t:C_SINR + 64 * t + 64]
                raw = STG[0][:, t, :].rearrange("p (h n) -> p h n", h=8)
                tmp = RTB[:, t, :].rearrange("p (h n) -> p h n", h=8)
                o = RRO[:, t, :].rearrange("p (h n) -> p h n", h=8)
                dve.tensor_tensor(o, raw, cosr, ALU.mult)
                dve.tensor_tensor(tmp[:, :, 0:32], raw[:, :, 32:64], sinr[:, 0:32].unsqueeze(1).to_broadcast([P, 8, 32]),
                                  ALU.mult)
                then(dve.tensor_tensor(tmp[:, :, 32:64], raw[:, :, 0:32],
                                       sinr[:, 32:64].unsqueeze(1).to_broadcast([P, 8, 32]), ALU.mult))
                dve.tensor_tensor(o, o, tmp, ALU.add).then_inc(sem("ret_rotated"), 1)

            dve.wait_ge(sem("in_by_act"), 4)
            dve.wait_ge(sem("in_by_dve"), 4)
            rotate(0)
            rotate(1)
            in_evac(4)
            scale0(4)
            scale0(5)
            for t in range(TT):
                dve.wait_ge(sem("rg_tanh"), t + 1)
                dve.scalar_tensor_tensor(out=GATE[:, t, :], in0=THR[:, t, :], scalar=1.0, in1=B[2 + t][:, :],
                                         op0=ALU.add, op1=ALU.mult).then_inc(sem("gate_ready"), 1)
            att_out0(1)
            dve.wait_ge(sem("rqk_turned"), 1)
            dve.tensor_copy(RT4[:, 0:2, :].rearrange("p c s -> p (c s)"), B[4][:, :]).then_inc(sem("rqkT_by_dve"), 1)
            dve.wait_ge(sem("decay_landed"), 16)
            for par in range(2):
                dve.wait_ge(sem("rs_ready"), par + 1)
                dve.tensor_tensor(RP0[:, 2 * par:2 * par + 2, :], B[4 + par][:, :].rearrange("p (h s) -> p h s", h=2),
                                  DEC[:, 2 * par:2 * par + 2, :], ALU.mult).then_inc(sem("rs_decayed"), 1)
            for par in range(2):
                dve.wait_ge(sem("rs_ready"), par + 3)
                dve.tensor_tensor(RP1[:, 2 * par:2 * par + 2, :], B[6 + par][:, 0:256].rearrange("p (h s) -> p h s", h=2),
                                  DEC[:, 2 * par:2 * par + 2, 0:P], ALU.mult).then_inc(sem("rs_decayed"), 1)
            for t in range(TT):
                dve.wait_ge(sem("ro_ready"), t + 1)
                for h in range(RH):
                    i = dve.bn_stats(BNS[:, t, h, :], B[t][:, h * RV:(h + 1) * RV])
            then(i)
            for t in range(TT):
                for h in range(RH):
                    i = dve.bn_aggr(BNA[:, t, h, :], BNS[:, t, h, :])
            then(i)
            dve.tensor_scalar(BNE.rearrange("p (t h) -> p t h", t=TT), BNA[:, :, :, 1], EPS, None, ALU.add)\
                .then_inc(sem("gn_ready"), 1)
            dve.wait_ge(sem("gn_rstd"), 1)
            for t in range(TT):
                for h in range(RH):
                    c = slice(h * RV, (h + 1) * RV)
                    i = dve.tensor_scalar(RET[:, t, c], B[t][:, c], BNA[:, t, h, 0:1], BNR[:, 4 * t + h:4 * t + h + 1],
                                          ALU.subtract, ALU.mult)
                then(i)
                dve.tensor_tensor(RET[:, t, :], RET[:, t, :], GATE[:, t, :], ALU.mult).then_inc(sem("ret_out"), 1)
            dve.wait_ge(sem("ret_out"), 2)
            dve.wait_ge(sem("mix0_turned"), 1)
            dve.tensor_copy(XT[:, 4:6, :].rearrange("p c s -> p (c s)"), B[6][:, :]).then_inc(sem("mix0T_by_dve"), 1)
            dve.wait_ge(sem("mix0_turned"), 3)
            dve.wait_ge(sem("gn_halved"), 1)
            dve.tensor_tensor(XT[:, 0:2, :], B[4][:, :].rearrange("p (k s) -> p k s", k=2),
                              GN[:, 0:2].unsqueeze(2).to_broadcast([P, 2, SEQ]), ALU.mult).then_inc(sem("mix0T_by_dve"), 1)
            for half in range(2):
                for t in range(TT):
                    dve.wait_ge(sem("out0_ready"), 2 * half + t + 1)
                    hh = H[:, t, half * 512:(half + 1) * 512]
                    dve.tensor_tensor(hh, hh, B[2 * half + t][:, :], ALU.add).then_inc(sem("h_updates"), 1)

            def experts(l, u0):
                kn = 3 * l + 1
                norm(kn)
                xt_evac(kn)
                for t in range(TT):
                    dve.wait_ge(sem("hs_high"), 2 * l + t + 1)
                    i = dve.tensor_tensor(HSP[1][:, t, :], HS[:, t, :], HSP[0][:, t, :].bitcast(F32), ALU.subtract)
                i.then_inc(sem("hs_low"), 1)
                t3 = lambda a, n: RT[:, a:a + 2 * n].rearrange("p (t n) -> p t n", t=TT)
                wide = lambda ap, n: ap.to_broadcast([P, TT, n])
                LG, LE = t3(140, 4), t3(148, 16)
                GB, GE, GX, GS, GOH = t3(20, 4), t3(28, 4), t3(36, 1), t3(38, 1), t3(40, 4)
                ES4, M1, EQ, MX, OH1 = t3(48, 4), t3(56, 1), t3(58, 4), t3(66, 1), t3(68, 4)
                OH2, SEC, W1, W2 = t3(76, 4), t3(84, 1), t3(86, 1), t3(88, 1)
                M2, GWT = t3(90, 1), t3(92, 1)
                M = t3(100, NE)
                O1, O2, EL, SLT = t3(180, NE), t3(212, NE), t3(244, NE), t3(276, NE)
                CNT, NBK, CI, NI, OFF = (RT[:, 308 + 16 * n:324 + 16 * n] for n in range(5))
                S1, S2 = t3(404, 1), t3(406, 1)
                OC, OFW = RT[:, 408:424], RT[:, 424:440]
                OVE, OVR, OVO, OVW, OC2 = (RT[:, 440 + 8 * n:448 + 8 * n] for n in range(5))
                MK, MK2 = RT[:, 180:196], RT[:, 196:212]
                rev = C[:, C_REV:C_REV + 4].unsqueeze(1).to_broadcast([P, TT, 4])
                dve.wait_ge(sem("logits_ready"), l + 1)
                lg = B[0][:, 0:40].rearrange("p (t n) -> p t n", t=TT)
                dve.tensor_tensor(LG, lg[:, :, 0:4], BR[:, l, 0:4].unsqueeze(1).to_broadcast([P, TT, 4]), ALU.add)
                then(dve.tensor_tensor(LE, lg[:, :, 4:20], BR[:, l, 4:20].unsqueeze(1).to_broadcast([P, TT, 16]), ALU.add))

                def first_max(val, mx, hot):
                    then(dve.tensor_reduce(mx, val, AX.X, ALU.max))
                    then(dve.tensor_tensor(EQ, val, wide(mx, 4), ALU.is_ge))
                    then(dve.tensor_tensor(EQ, EQ, rev, ALU.mult))
                    then(dve.tensor_reduce(MX, EQ, AX.X, ALU.max))
                    then(dve.tensor_tensor(hot, EQ, wide(MX, 4), ALU.is_equal))

                first_max(LG, GX, GOH)
                dve.tensor_tensor(GB, LG, wide(GX, 4), ALU.subtract).then_inc(sem("g_below_max"), 1)
                then(dve.tensor_tensor(EL.rearrange("p t (g e) -> p t g e", g=G), LE.rearrange("p t (g e) -> p t g e", g=G),
                                       GOH.unsqueeze(3).to_broadcast([P, TT, G, E]), ALU.mult))
                then(dve.tensor_reduce(ES4, EL.rearrange("p t (g e) -> p t e g", g=G), AX.X, ALU.add))
                first_max(ES4, M1, OH1)
                then(dve.scalar_tensor_tensor(out=ES4, in0=OH1, scalar=NEG, in1=ES4, op0=ALU.mult, op1=ALU.add))
                first_max(ES4, M2, OH2)
                dve.tensor_tensor(SEC, M2, M1, ALU.subtract).then_inc(sem("second_below_first"), 1)
                for oh, o in ((OH1, O1), (OH2, O2)):
                    for t in range(TT):
                        i = dve.tensor_tensor(o[:, t, :].rearrange("p (g e) -> p g e", g=G),
                                              GOH[:, t, :].unsqueeze(2).to_broadcast([P, G, E]),
                                              oh[:, t, :].unsqueeze(1).to_broadcast([P, G, E]), ALU.mult)
                then(i)
                dve.tensor_tensor(M, O1, O2, ALU.add).then_inc(sem("chosen"), 1)
                dve.wait_ge(sem("g_exp"), l + 1)
                then(dve.tensor_reduce(GS, GB, AX.X, ALU.add))
                then(dve.reciprocal(GWT, GS))
                dve.wait_ge(sem("second_exp"), l + 1)
                then(dve.tensor_scalar(W1, SEC, 1.0, None, ALU.add))
                then(dve.reciprocal(W1, W1))
                then(dve.tensor_tensor(W1, W1, GWT, ALU.mult))
                then(dve.tensor_tensor(W2, W1, SEC, ALU.mult))
                dve.wait_ge(sem("ranks_ready"), l + 1)
                then(dve.tensor_copy(CNT, B[1][:, 32:48]))
                ones = C[:, C_ONE:C_ONE + NE]
                then(dve.tensor_tensor_scan(CI, ones, CNT, 0.0, ALU.mult, ALU.add))
                then(dve.tensor_tensor(OFF, CI, CNT, ALU.subtract))
                then(dve.tensor_tensor(SLT, B[1][:, 0:32].rearrange("p (t e) -> p t e", t=TT),
                                       OFF.unsqueeze(1).to_broadcast([P, TT, NE]), ALU.add))
                then(dve.tensor_tensor(O1, O1, SLT, ALU.mult))
                then(dve.tensor_reduce(S1, O1, AX.X, ALU.add))
                then(dve.tensor_tensor(O2, O2, SLT, ALU.mult))
                dve.tensor_reduce(S2, O2, AX.X, ALU.add).then_inc(sem("slots_ready"), 1)
                dve.wait_ge(sem("slots_ready"), l + 1)
                dve.wait_ge(sem("iota_ready"), l + 1)
                for t in range(TT):
                    i = dve.tensor_scalar(TMP[:, t, :], IOTA, S2[:, t, :], None, ALU.is_equal)
                then(i)
                for t in range(TT):
                    i = dve.scalar_tensor_tensor(out=PH[:, t, :], in0=IOTA, scalar=S1[:, t, :], in1=TMP[:, t, :],
                                                 op0=ALU.is_equal, op1=ALU.add)
                i.then_inc(sem("onehots_ready"), 1)
                one = slice(0, 1)
                then(dve.tensor_scalar(OFW, OFF, float(LAST), None, ALU.min))
                dve.tensor_copy(TBL[0:1, 0:NE], OFW[one]).then_inc(sem("table_ready"), 1)
                for t in range(TT):
                    dve.tensor_scalar(GM[:, t, :], IOTA, S2[:, t, :], W2[:, t, :], ALU.is_equal, ALU.mult)
                    then(dve.tensor_scalar(TMP[:, t, :], IOTA, S1[:, t, :], W1[:, t, :], ALU.is_equal, ALU.mult))
                    i = dve.tensor_tensor(GM[:, t, :], GM[:, t, :], TMP[:, t, :], ALU.add)
                i.then_inc(sem("gates_ready"), 1)

                def row_slots(oc, start, first, end, valid, tmp):
                    then(dve.tensor_scalar(oc, start, C[:, C_PM:C_PM + 1], None, ALU.add))
                    dve.tensor_tensor(valid, oc, first, ALU.is_ge)
                    then(dve.tensor_tensor(tmp, oc, end, ALU.is_lt))
                    then(dve.tensor_tensor(valid, valid, tmp, ALU.mult))
                    then(dve.scalar_tensor_tensor(out=oc, in0=oc, scalar=1.0, in1=valid, op0=ALU.add, op1=ALU.mult))
                    then(dve.tensor_scalar(oc, oc, 1.0, None, ALU.subtract))

                row_slots(OC, OFW, OFF, CI, MK, MK2)

                def low(n, lap, e, m, chunks=range(NCH)):
                    at = lambda c: c if lap is None else lap * 16 + c
                    s, w = landed(n)
                    dve.wait_ge(s, at(w))
                    for c in chunks:
                        dve.wait_ge(sem("hi_split"), at(8 * (NE * l + e) + 4 * m + c + 1))
                        dve.tensor_tensor(HL[:, c, 1, :, :].rearrange("p k f -> p (k f)"),
                                          unit(n)[:, c * 1024:(c + 1) * 1024],
                                          HL[:, c, 0, :, :].rearrange("p k f -> p (k f)").bitcast(F32), ALU.subtract)\
                            .then_inc(sem("lo_split"), 1)

                def rows(e, lap):
                    off = dve.value_load(TBL[0:1, bass.ds(e if lap is None else lap * 2 + e, 1)], min_val=0, max_val=LAST)
                    dve.wait_ge(sem("xh_ready"), NE * l + e + 1 if lap is None else lap * 2 + (NE * l + e + 1))
                    dve.tensor_tensor(XHL[:, e % 2, :, BLK:P], XS[:, :, bass.ds(off, BLK)],
                                      XHL[:, e % 2, :, 0:BLK].bitcast(F32), ALU.subtract).then_inc(sem("xl_ready"), 1)

                def gated(off, done):
                    dve.tensor_tensor(ACTT, B[6][:, 0:KF * BLK].rearrange("p (f s) -> p f s", f=KF),
                                      GR[:, bass.ds(off, BLK)].unsqueeze(1).to_broadcast([P, KF, BLK]), ALU.mult)\
                        .then_inc(done, 1)

                def onehots(par, col, first, value, done):
                    dve.tensor_scalar(PTMP, SROW[:, 0, :], col, None, ALU.is_equal).then_inc(first, 1)
                    dve.wait_ge(first, value)
                    dve.scalar_tensor_tensor(out=PT2[:, par, :], in0=SROW[:, 1, :], scalar=col, in1=PTMP,
                                             op0=ALU.is_equal, op1=ALU.add).then_inc(done, 1)

                def outputs(high_ready, done, value):
                    for half in range(2):
                        c = slice(half * 512, (half + 1) * 512)
                        dve.wait_ge(high_ready, value(half))
                        dve.tensor_tensor(Y2[BLK:P, c], B[6 + half][0:BLK, :], Y2[0:BLK, c].bitcast(F32), ALU.subtract)\
                            .then_inc(done, 1)

                low(u0, None, 0, 0, (0, 1))
                for k in (6, 7, 2, 3):
                    dve.wait_ge(sem("rows_ready"), 8 * l + (k - 3 if k > 3 else 8))
                    dve.tensor_scalar(XS[:, k, :], B[k][:, :], NW[:, kn, k:k + 1], None, ALU.mult).then_inc(sem("rows_by_dve"), 1)
                dve.wait_ge(sem("rows_by_dve"), 4 * (l + 1))
                dve.wait_ge(sem("rows_by_act"), 4 * (l + 1))
                rows(0, None)
                low(u0, None, 0, 0, (2, 3))

                def step(e, lap):
                    def v(per, const):
                        c = per * (NE * l + e) + const
                        return c if lap is None else lap * (2 * per) + c
                    later = l + e > 1 or lap is not None
                    if e < NE:
                        low(u0 + 3 * e + 1, lap, e, 1)
                    if 1 <= e <= NE:
                        off = dve.value_load(TBL[0:1, bass.ds(e - 1 if lap is None else lap * 2 + (e - 1), 1)],
                                             min_val=0, max_val=LAST)
                        dve.wait_ge(sem("gr_copied"), l + 1)
                        dve.wait_ge(sem("act_turned"), v(1, 0))
                        if later:
                            dve.wait_ge(sem("y_ready"), v(2, -2))
                        gated(off, sem("actt_ready"))
                    if e < NE:
                        dve.wait_ge(sem("gate_low"), v(1, 1))
                        dve.tensor_tensor(GSUM, B[4][0:BLK, :], TG, ALU.add).then_inc(sem("gate_folded"), 1)
                        dve.wait_ge(sem("th_ready"), v(1, 1))
                        dve.scalar_tensor_tensor(out=AG, in0=TH, scalar=1.0, in1=GSUM, op0=ALU.add, op1=ALU.mult)\
                            .then_inc(sem("ag_ready"), 1)
                        dve.wait_ge(sem("up_low"), v(1, 1))
                        dve.tensor_tensor(US, B[5][0:BLK, :], TU, ALU.add).then_inc(sem("up_folded"), 1)
                        dve.wait_ge(sem("up_folded"), v(1, 1))
                        dve.wait_ge(sem("ag_ready"), v(1, 1))
                        dve.tensor_tensor(US, AG, US, ALU.mult).then_inc(sem("act_ready"), 1)
                        if e < NE - 1:
                            rows(e + 1, lap)
                            low(u0 + 3 * e + 3, lap, e + 1, 0)
                        if l * NE + e >= 2:
                            dve.wait_ge(sem("sc_done"), v(1, -1))
                        onehots(e % 2, OC[:, bass.ds(e if lap is None else lap * 2 + e, 1)], sem("first_onehots"), v(1, 1),
                                sem("pt2_ready"))
                    if 1 <= e <= NE:
                        outputs(sem("yh_ready"), sem("yl_ready"), lambda half: v(2, half - 1))

                step(0, None)
                for e in range(1, 4):
                    step(e, None)
                with dve.Fori(0, 5) as i:
                    step(4, i)
                    step(5, i)
                step(14, None)
                g3 = [g.rearrange("p (b e) -> p b e", b=MAXOV) for g in GRID]
                wide_e = lambda a: a.unsqueeze(1).to_broadcast([P, MAXOV, NE])
                then(dve.tensor_scalar(NBK, CNT, float(BLK), None, ALU.is_gt))
                for n in range(2, SEQ // BLK):
                    then(dve.scalar_tensor_tensor(out=NBK, in0=CNT, scalar=float(n * BLK), in1=NBK,
                                                  op0=ALU.is_gt, op1=ALU.add))
                then(dve.tensor_tensor_scan(NI, ones, NBK, 0.0, ALU.mult, ALU.add))
                then(dve.tensor_tensor(NBK, NI, NBK, ALU.subtract))
                dve.wait_ge(sem("grids_ready"), 2 * (l + 1))
                then(dve.tensor_tensor(g3[2], g3[0], wide_e(NBK), ALU.is_ge))
                then(dve.tensor_tensor(g3[3], g3[0], wide_e(NI), ALU.is_lt))
                then(dve.tensor_tensor(g3[2], g3[2], g3[3], ALU.mult))
                then(dve.tensor_tensor(g3[3], g3[2], g3[1], ALU.mult))
                then(dve.tensor_reduce(OVE, g3[3], AX.X, ALU.add))
                then(dve.tensor_tensor(g3[3], g3[2], wide_e(CI), ALU.mult))
                then(dve.tensor_reduce(OVR, g3[3], AX.X, ALU.add))
                then(dve.tensor_tensor(g3[3], g3[0], wide_e(NBK), ALU.subtract))
                then(dve.scalar_tensor_tensor(out=g3[3], in0=g3[3], scalar=float(BLK), in1=wide_e(OFF),
                                              op0=ALU.mult, op1=ALU.add))
                then(dve.tensor_tensor(g3[3], g3[3], g3[2], ALU.mult))
                then(dve.tensor_reduce(OVO, g3[3], AX.X, ALU.add))
                then(dve.tensor_scalar(OVO, OVO, float(BLK), None, ALU.add))
                then(dve.tensor_scalar(OVW, OVO, float(LAST), None, ALU.min))
                dve.tensor_copy(TBL[0:1, 16:17], NI[one, NE - 1:NE])
                dve.tensor_copy(TBL[0:1, 17:17 + MAXOV], OVW[one])
                dve.tensor_copy(TBL[0:1, 17 + MAXOV:17 + 2 * MAXOV], OVE[one]).then_inc(sem("table_ready"), 1)
                row_slots(OC2, OVW, OVO, OVR, OVO, OVR)
                for e in (15, 16):
                    step(e, None)

                dve.wait_ge(sem("table_ready"), 2 * l + 2)
                novf = dve.value_load(TBL[0:1, 16:17], min_val=0, max_val=MAXOV - 1)
                with dve.If(novf > 0):
                    dve.wait_ge(sem("sc_done"), NE * (l + 1))
                    with dve.Fori(0, novf) as b:
                        off = dve.value_load(TBL[0:1, bass.ds(b + 17, 1)], min_val=0, max_val=LAST)
                        ov_wait(dve, l, b, "tanh")
                        dve.scalar_tensor_tensor(out=AG, in0=TH, scalar=1.0, in1=B[4][0:BLK, :], op0=ALU.add, op1=ALU.mult)\
                            .then_inc(ov_sem(l, "vectors"), 1)
                        ov_wait(dve, l, b, "ag")
                        ov_wait(dve, l, b, "up")
                        dve.tensor_tensor(US, AG, B[5][0:BLK, :], ALU.mult).then_inc(ov_sem(l, "vectors"), 1)
                        onehots(0, OC2[:, bass.ds(b, 1)], ov_sem(l, "vectors"), ov_count(b, "first_onehots")[1], ov_sem(l, "vectors"))
                        ov_wait(dve, l, b, "turned")
                        gated(off, ov_sem(l, "vectors"))
                        outputs(ov_sem(l, "copies"), ov_sem(l, "vectors"), lambda half: ov_count(b, ("high_left", "high_right")[half])[1])
                dve.wait_ge(sem("moe_ready"), l + 1)
                for t in range(TT):
                    for half in range(2):
                        hh = H[:, t, half * 512:(half + 1) * 512]
                        dve.tensor_tensor(hh, hh, B[2 * t + half][:, :], ALU.add).then_inc(sem("h_updates"), 1)

            def ple(l):
                norm(3 * l + 2)
                xt_evac(3 * l + 2)
                dve.wait_ge(sem("pp_ready"), l + 1)
                for half in range(2):
                    for t in range(TT):
                        dve.wait_ge(sem("pg_tanh"), 4 * l + 2 * half + t + 1)
                        c = slice(half * 512, (half + 1) * 512)
                        then(dve.scalar_tensor_tensor(out=THG[:, t, c], in0=THG[:, t, c], scalar=1.0,
                                                      in1=B[2 * t + half][:, :], op0=ALU.add, op1=ALU.mult))
                        dve.scalar_tensor_tensor(out=H[:, t, c], in0=THG[:, t, c], scalar=0.5, in1=H[:, t, c],
                                                 op0=ALU.mult, op1=ALU.add).then_inc(sem("h_updates"), 1)

            experts(0, U_MOE0)
            ple(0)

            norm(3)
            xt_evac(3)
            dve.wait_ge(sem("bq_landed"), 16)
            for u in range(2):
                for t in range(TT):
                    dve.wait_ge(sem("qkv_ready"), 2 * u + t + 1)
                    dve.tensor_tensor(Q1[:, t, 512 * u:512 * u + 512], B[2 * u + t][:, :], BQ[:, 512 * u:512 * u + 512],
                                      ALU.add)
            for t in range(TT):
                dve.wait_ge(sem("qkv_ready"), 4 + t + 1)
                then(dve.tensor_tensor(KV[:, t, :], B[4 + t][:, 0:256], BQ[:, 1024:1280], ALU.add))
            for t in range(TT):
                for a, n, h0 in ((Q1[:, t, :], SH, 0), (KV[:, t, 0:128], SKV, SH)):
                    v = a.rearrange("p (h n) -> p h n", h=n)
                    cs = C[:, C_COSO + ROT * t:C_COSO + ROT * (t + 1)].unsqueeze(1).to_broadcast([P, n, ROT])
                    si = C[:, C_SINO + ROT * t:C_SINO + ROT * (t + 1)]
                    tmp = RB1[:, t, h0:h0 + n, :]
                    dve.tensor_tensor(tmp[:, :, 0:8], v[:, :, 8:16], si[:, 0:8].unsqueeze(1).to_broadcast([P, n, 8]), ALU.mult)
                    then(dve.tensor_tensor(tmp[:, :, 8:16], v[:, :, 0:8],
                                           si[:, 8:16].unsqueeze(1).to_broadcast([P, n, 8]), ALU.mult))
                    then(dve.tensor_tensor(v[:, :, 0:ROT], v[:, :, 0:ROT], cs, ALU.mult))
                    then(dve.tensor_tensor(v[:, :, 0:ROT], v[:, :, 0:ROT], tmp, ALU.add))
                dve.tensor_copy(KDUP[:, t, :, 0, :], KV[:, t, 0:128].rearrange("p (g n) -> p g n", g=SKV))
                dve.tensor_copy(KDUP[:, t, :, 1, :], KV[:, t, 0:128].rearrange("p (g n) -> p g n", g=SKV))\
                    .then_inc(sem("q1_rotated"), 1)
            dve.wait_ge(sem("q1_turned"), 1)
            dve.tensor_copy(Q1T[:, 0:2, :].rearrange("p c s -> p (c s)"), B[6][:, :]).then_inc(sem("q1T_by_dve"), 1)
            dve.wait_ge(sem("q1_turned"), 3)
            dve.tensor_copy(Q1T[:, 4:6, :].rearrange("p c s -> p (c s)"), B[0][:, :]).then_inc(sem("q1T_by_dve"), 1)
            dve.wait_ge(sem("k1_turned"), 1)
            dve.tensor_copy(K1T.rearrange("p g s -> p (g s)"), B[2][:, :]).then_inc(sem("k1T_copied"), 1)

            def scale1(g):
                t, heads = odd_heads(g)
                nh, keys, h0 = len(heads), (128, 192)[t], heads[0]
                dve.wait_ge(sem("s1_ready"), g + 1)
                if g >= 2:
                    dve.wait_ge(sem("pt1_ready"), g - 1)
                if t == 0:
                    sc = SC1[g % 2].rearrange("p (h s) -> p h s", h=nh)
                else:
                    full = SC1[g % 2].rearrange("p (h s) -> p h s", h=nh)
                    sc = full[:, :, 64:256]
                    if g < 6:
                        dve.memset(full[:, :, 0:64], 0.0)
                mask = C[:, C_M0:C_M0 + P] if t == 0 else C[:, C_M1:C_M1 + 192]
                dve.scalar_tensor_tensor(out=sc, in0=B[4 + g % 2][:, 0:nh * keys].rearrange("p (h s) -> p h s", h=nh),
                                         scalar=HD ** -0.5, in1=mask.unsqueeze(1).to_broadcast([P, nh, keys]),
                                         op0=ALU.mult, op1=ALU.add).then_inc(sem("s1_scaled"), 1)
                dve.wait_ge(sem("s1_scaled"), g + 1)
                hs = slice(h0, h0 + 2 * nh - 1, 2)
                then(dve.tensor_reduce(SM[:, t, hs], sc, AX.X, ALU.max))
                then(dve.tensor_tensor(SM[:, t, hs], SM[:, t, hs], SK[:, hs], ALU.max))
                dve.tensor_scalar(SM[:, t, hs], SM[:, t, hs], -1.0, None, ALU.mult).then_inc(sem("max1_ready"), 1)

            def att_out1(t):
                dve.wait_ge(sem("max1_ready"), (4, 12)[t])
                dve.tensor_tensor(ES[:, t, :], SM[:, t, :], SK[:, :], ALU.add).then_inc(sem("sink_below_max"), 1)
                dve.wait_ge(sem("sink_exp"), t + 1)
                dve.wait_ge(sem("s1_exp"), SH * (t + 1))
                then(dve.tensor_tensor(SM[:, 2 + t, :], SM[:, 2 + t, :], ES[:, t, :], ALU.add))
                then(dve.reciprocal(SM[:, 2 + t, :], SM[:, 2 + t, :]))
                dve.wait_ge(sem("pv1_ready"), (4, 12)[t])
                for n in range(2):
                    i = dve.tensor_tensor(MIX1[:, t, 512 * n:512 * n + 512].rearrange("p (h n) -> p h n", h=8),
                                          B[2 * t + n][:, :].rearrange("p (h n) -> p h n", h=8),
                                          SM[:, 2 + t, 8 * n:8 * n + 8].unsqueeze(2).to_broadcast([P, 8, HD]), ALU.mult)
                i.then_inc(sem("att1_out"), 1)

            for g in range(12):
                scale1(g)
            dve.wait_ge(sem("bo_landed"), 16)
            for t in range(TT):
                then(dve.tensor_tensor(H[:, t, :], H[:, t, :], BO, ALU.add))
            att_out1(0)
            att_out1(1)
            for q in (0, 2):
                dve.wait_ge(sem("mix1_turned"), q + 1)
                dve.tensor_copy(XT[:, 2 * q:2 * q + 2, :].rearrange("p c s -> p (c s)"), B[4 + q][:, :])\
                    .then_inc(sem("mix1T_by_dve"), 1)
            for half in range(2):
                for t in range(TT):
                    dve.wait_ge(sem("out1_ready"), 2 * half + t + 1)
                    hh = H[:, t, half * 512:(half + 1) * 512]
                    dve.tensor_tensor(hh, hh, B[2 * half + t][:, :], ALU.add).then_inc(sem("h_updates"), 1)
            experts(1, U_MOE1)
            ple(1)
            norm(6)
            dve.wait_ge(sem("fw_landed"), 16)
            for t in range(TT):
                dve.scalar_tensor_tensor(out=OUTB[:, t, :], in0=H[:, t, :], scalar=ST[:, 4 + t:5 + t], in1=FW,
                                         op0=ALU.mult, op1=ALU.mult).then_inc(sem("out_ready"), 1)


_INS = ["x", "p", "norm_mix", "norm_ffn", "norm_ple", "final_norm", "even_w_in", "even_ret_gn", "even_rel_bias",
        "even_w_out", "odd_w_qkv", "odd_b_qkv", "odd_sinks", "odd_w_out", "odd_b_out", "moe_w_group", "moe_b_group",
        "moe_w_router", "moe_b_router", "moe_w_gate", "moe_w_up", "moe_w_down", "ple_w_proj", "ple_w_gate"]


def kernel(**inputs):
    import concourse.bacc as bacc
    from concourse.bass_utils import run_bass_kernel_spmd

    nc = bacc.Bacc("TRN2", target_bir_lowering=False, num_devices=1)
    const, decay = constants()
    flip = np.ascontiguousarray(np.eye(P, dtype=np.float32)[::-1])
    arrays, args = {}, []
    for name, a in [(n, inputs[n]) for n in _INS] + [("const", const), ("decay", decay), ("flip", flip)]:
        a = np.ascontiguousarray(a)
        arrays[f"in_{name}_dram"] = a
        args.append(nc.dram_tensor(f"in_{name}_dram", a.shape, mybir.dt.from_np(a.dtype), kind="ExternalInput").ap())
    args.append(nc.dram_tensor("out_0_dram", (1, SEQ, D), F32, kind="ExternalOutput").ap())
    args.append(nc.dram_tensor("rel_rows_dram", (CH, REL_W), F32, kind="Internal").ap())
    build(nc, *args)
    r = run_bass_kernel_spmd(nc, [arrays], core_ids=[0])
    return r.results[0]["out_0_dram"]
```
